# Optimizing a Trainium2 kernel written in Bass

```python
import jax, jax.numpy as jnp
from jax import lax
import numpy as np

D_MODEL = 1024
BATCH = 1
SEQ = 1024
DEPTH = 1

GLA_HEADS = 4
GLA_DK = 64
GLA_DV = 128
GLA_GATE_RANK = 16
GLA_GATE_TAU = 16.0
GLA_CHUNK = 64
DIFF_HEADS = 4
DIFF_DH = 64
DIFF_DV = 2 * DIFF_DH
ROPE_THETA = 500000.0
ROPE_DIM = DIFF_DH // 4
Q_BLOCK = 128
NEG_INF = -1e30
GLA_QK_W = GLA_HEADS * GLA_DK
GLA_V_W = GLA_HEADS * GLA_DV
DIFF_QK_W = DIFF_HEADS * 2 * DIFF_DH
DIFF_V_W = DIFF_HEADS * DIFF_DV
IN_SIZES = (GLA_QK_W, GLA_QK_W, GLA_V_W, GLA_V_W, GLA_GATE_RANK,
            DIFF_QK_W, DIFF_QK_W, DIFF_V_W, D_MODEL, D_MODEL)
D_IN = sum(IN_SIZES)
N_GROUPS = 4
EXPERTS_PER_GROUP = 8
N_EXPERTS = N_GROUPS * EXPERTS_PER_GROUP
TOP_K = 2
D_EXPERT = 512
MOE_BLOCK = 128
NORM_EPS = 1e-6
N_MOD = 6

kernel_name = "hybrid_gla_diffattn_hmoe_block"

def rms_norm(x, gain):
    xf = x.astype(jnp.float32)
    y = xf * lax.rsqrt(jnp.mean(xf * xf, axis=-1, keepdims=True) + NORM_EPS)
    return (y * gain.astype(jnp.float32)).astype(x.dtype)

def rope_tables(positions):
    half = ROPE_DIM // 2
    inv_freq = ROPE_THETA ** (-jnp.arange(half, dtype=jnp.float32) / half)
    ang = positions.astype(jnp.float32)[:, :, None] * inv_freq
    return jnp.cos(ang)[:, :, None, None, :], jnp.sin(ang)[:, :, None, None, :]

def partial_rope(x, cos, sin):
    half = ROPE_DIM // 2
    xr = x[..., :ROPE_DIM].astype(jnp.float32)
    x1, x2 = xr[..., :half], xr[..., half:]
    rot = jnp.concatenate([x1 * cos - x2 * sin, x2 * cos + x1 * sin], axis=-1)
    return jnp.concatenate([rot.astype(x.dtype), x[..., ROPE_DIM:]], axis=-1)

def gla_chunked(q, k, v, log_a):
    B, S, H, _ = q.shape
    N = S // GLA_CHUNK
    def to_chunks(t):
        return t.astype(jnp.float32).reshape(B, N, GLA_CHUNK, H, -1).transpose(0, 3, 1, 2, 4)
    q, k, v, g = to_chunks(q), to_chunks(k), to_chunks(v), to_chunks(log_a)
    b = jnp.cumsum(g, axis=3)
    b_last = b[:, :, :, -1:, :]
    q_in = q * jnp.exp(b)
    k_in = k * jnp.exp(-b)
    causal = jnp.tril(jnp.ones((GLA_CHUNK, GLA_CHUNK), dtype=bool))
    att = jnp.where(causal, jnp.einsum('bhnck,bhnsk->bhncs', q_in, k_in), 0.0)
    o_intra = jnp.einsum('bhncs,bhnsv->bhncv', att, v)
    s_chunk = jnp.einsum('bhnsk,bhnsv->bhnkv', k * jnp.exp(b_last - b), v)
    decay = jnp.exp(b_last[:, :, :, 0, :])

    def step(state, inp):
        d, s_c = inp
        return state * d[..., None] + s_c, state

    init = jnp.zeros((B, H, GLA_DK, GLA_DV), jnp.float32)
    _, s_prev = lax.scan(step, init, (jnp.moveaxis(decay, 2, 0), jnp.moveaxis(s_chunk, 2, 0)))
    s_prev = jnp.moveaxis(s_prev, 0, 2)
    o = o_intra + jnp.einsum('bhnck,bhnkv->bhncv', q_in, s_prev)
    return o.transpose(0, 2, 3, 1, 4).reshape(B, S, H, GLA_DV)

def gla_branch(q, k, v, r, a_lr, alpha_up, alpha_b, out_g):
    B, S, _ = q.shape
    q = q.reshape(B, S, GLA_HEADS, GLA_DK) * (GLA_DK ** -0.5)
    k = k.reshape(B, S, GLA_HEADS, GLA_DK)
    v = v.reshape(B, S, GLA_HEADS, GLA_DV)
    log_a = jax.nn.log_sigmoid((a_lr @ alpha_up + alpha_b).astype(jnp.float32)) / GLA_GATE_TAU
    o = gla_chunked(q, k, v, log_a.reshape(B, S, GLA_HEADS, GLA_DK)).astype(v.dtype)
    o = rms_norm(o, out_g) * jax.nn.silu(r.reshape(B, S, GLA_HEADS, GLA_DV))
    return o.reshape(B, S, GLA_V_W)

def diff_branch(q, k, v, cos, sin, q_g, k_g, lq1, lk1, lq2, lk2, out_g, lambda_init):
    B, S, _ = q.shape
    q = partial_rope(rms_norm(q.reshape(B, S, DIFF_HEADS, 2, DIFF_DH), q_g), cos, sin)
    k = partial_rope(rms_norm(k.reshape(B, S, DIFF_HEADS, 2, DIFF_DH), k_g), cos, sin)
    q = q.transpose(0, 2, 3, 1, 4)
    k = k.transpose(0, 2, 3, 1, 4)
    v = v.reshape(B, S, DIFF_HEADS, DIFF_DV).transpose(0, 2, 1, 3)
    f32 = jnp.float32
    lam = (jnp.exp(jnp.sum(lq1.astype(f32) * lk1.astype(f32)))
           - jnp.exp(jnp.sum(lq2.astype(f32) * lk2.astype(f32))) + lambda_init)
    n_blk = S // Q_BLOCK
    qb = q.reshape(B, DIFF_HEADS, 2, n_blk, Q_BLOCK, DIFF_DH).transpose(3, 0, 1, 2, 4, 5)
    key_idx = jnp.arange(S)
    scale = DIFF_DH ** -0.5

    def one_block(args):
        q_blk, blk = args
        s = jnp.einsum('bhcqd,bhckd->bhcqk', q_blk, k, preferred_element_type=f32) * scale
        q_idx = blk * Q_BLOCK + jnp.arange(Q_BLOCK)
        s = jnp.where(key_idx[None, :] <= q_idx[:, None], s, NEG_INF)
        p = jax.nn.softmax(s, axis=-1)
        a = p[:, :, 0] - lam * p[:, :, 1]
        return jnp.einsum('bhqk,bhkv->bhqv', a.astype(v.dtype), v)

    o = lax.map(one_block, (qb, jnp.arange(n_blk)))
    o = o.transpose(1, 0, 3, 2, 4).reshape(B, S, DIFF_HEADS, DIFF_DV)
    o = rms_norm(o, out_g) * (1.0 - lambda_init)
    return o.reshape(B, S, DIFF_V_W)

def hier_moe(h, w_rg, b_rg, w_re, b_re, w1, w3, w2):
    B, S, D = h.shape
    T = B * S
    xf = h.reshape(T, D)
    p_g = jax.nn.softmax((xf @ w_rg + b_rg).astype(jnp.float32), axis=-1)
    p_top, g_idx = lax.top_k(p_g, 1)
    e_logits = (xf @ w_re + b_re).astype(jnp.float32).reshape(T, N_GROUPS, EXPERTS_PER_GROUP)
    e_in = e_logits[jnp.arange(T), g_idx[:, 0]]
    pe_top, e_loc = lax.top_k(jax.nn.softmax(e_in, axis=-1), TOP_K)
    pe_top = pe_top / jnp.sum(pe_top, axis=-1, keepdims=True)
    weights = p_top * pe_top
    expert_ids = g_idx * EXPERTS_PER_GROUP + e_loc
    A = T * TOP_K
    flat_e = expert_ids.reshape(A)
    flat_tok = jnp.repeat(jnp.arange(T, dtype=jnp.int32), TOP_K)
    flat_w = weights.reshape(A)
    order = jnp.argsort(flat_e)
    sorted_e = flat_e[order]
    counts = jnp.bincount(flat_e, length=N_EXPERTS)
    starts = jnp.cumsum(counts) - counts
    padded = ((counts + MOE_BLOCK - 1) // MOE_BLOCK) * MOE_BLOCK
    pad_ends = jnp.cumsum(padded)
    pad_starts = pad_ends - padded
    dest = pad_starts[sorted_e] + (jnp.arange(A) - starts[sorted_e])
    NB = (A + N_EXPERTS * (MOE_BLOCK - 1) + MOE_BLOCK - 1) // MOE_BLOCK
    P = NB * MOE_BLOCK
    slot_tok = jnp.full((P,), T, jnp.int32).at[dest].set(flat_tok[order])
    slot_w = jnp.zeros((P,), jnp.float32).at[dest].set(flat_w[order])
    block_e = jnp.minimum(jnp.searchsorted(pad_ends, jnp.arange(NB) * MOE_BLOCK, side='right'),
                          N_EXPERTS - 1)
    x_pad = jnp.concatenate([xf, jnp.zeros((1, D), xf.dtype)], axis=0)
    xb = x_pad[slot_tok].reshape(NB, MOE_BLOCK, D)

    def expert_block(args):
        xi, e = args
        return (jax.nn.silu(xi @ w1[e]) * (xi @ w3[e])) @ w2[e]

    yb = lax.map(expert_block, (xb, block_e)).reshape(P, D)
    yb = (yb * slot_w[:, None]).astype(h.dtype)
    out = jnp.zeros((T + 1, D), h.dtype).at[slot_tok].add(yb)[:T]
    return out.reshape(B, S, D)

def setup_inputs(seed: int = 0) -> dict:
    key = jax.random.key(seed)
    ks = jax.random.split(key, 32)
    L, D = DEPTH, D_MODEL
    def nrm(k, shape, scale):
        return jax.random.normal(k, shape, jnp.float32) * scale
    def gain(k, shape):
        return 1.0 + 0.01 * jax.random.normal(k, shape, jnp.float32)
    offsets = jax.random.randint(ks[2], (BATCH, 1), 0, 1024, dtype=jnp.int32)
    return {
        "x": nrm(ks[0], (BATCH, SEQ, D), 1.0),
        "c": nrm(ks[1], (BATCH, D), 1.0),
        "positions": offsets + jnp.arange(SEQ, dtype=jnp.int32)[None, :],
        "ada_w": nrm(ks[3], (L, D, N_MOD * D), D ** -0.5),
        "ada_b": nrm(ks[4], (L, N_MOD * D), 0.02),
        "norm1_g": gain(ks[5], (L, D)),
        "norm2_g": gain(ks[6], (L, D)),
        "w_in": nrm(ks[7], (L, D, D_IN), D ** -0.5),
        "gla_alpha_up": nrm(ks[8], (L, GLA_GATE_RANK, GLA_QK_W), GLA_GATE_RANK ** -0.5),
        "gla_alpha_b": nrm(ks[9], (L, GLA_QK_W), 0.1),
        "gla_out_g": gain(ks[10], (L, GLA_DV)),
        "diff_q_g": gain(ks[11], (L, DIFF_DH)),
        "diff_k_g": gain(ks[12], (L, DIFF_DH)),
        "diff_lq1": nrm(ks[13], (L, DIFF_DH), 0.1),
        "diff_lk1": nrm(ks[14], (L, DIFF_DH), 0.1),
        "diff_lq2": nrm(ks[15], (L, DIFF_DH), 0.1),
        "diff_lk2": nrm(ks[16], (L, DIFF_DH), 0.1),
        "diff_out_g": gain(ks[17], (L, DIFF_DV)),
        "w_branch_a": nrm(ks[18], (L, GLA_V_W, D), GLA_V_W ** -0.5),
        "w_branch_b": nrm(ks[19], (L, DIFF_V_W, D), DIFF_V_W ** -0.5),
        "w_out": nrm(ks[20], (L, D, D), D ** -0.5),
        "router_group_w": nrm(ks[21], (L, D, N_GROUPS), D ** -0.5),
        "router_group_b": nrm(ks[22], (L, N_GROUPS), 0.01),
        "router_expert_w": nrm(ks[23], (L, D, N_EXPERTS), D ** -0.5),
        "router_expert_b": nrm(ks[24], (L, N_EXPERTS), 0.01),
        "expert_w1": nrm(ks[25], (L, N_EXPERTS, D, D_EXPERT), D ** -0.5),
        "expert_w3": nrm(ks[26], (L, N_EXPERTS, D, D_EXPERT), D ** -0.5),
        "expert_w2": nrm(ks[27], (L, N_EXPERTS, D_EXPERT, D), D_EXPERT ** -0.5),
    }

def reference(x, c, positions, ada_w, ada_b, norm1_g, norm2_g, w_in, gla_alpha_up, gla_alpha_b,
              gla_out_g, diff_q_g, diff_k_g, diff_lq1, diff_lk1, diff_lq2, diff_lk2, diff_out_g,
              w_branch_a, w_branch_b, w_out, router_group_w, router_group_b, router_expert_w,
              router_expert_b, expert_w1, expert_w3, expert_w2):
    B, S, D = x.shape
    cos, sin = rope_tables(positions)
    c_act = jax.nn.silu(c)
    split_idx = np.cumsum(IN_SIZES)[:-1].tolist()
    for l in range(DEPTH):
        lambda_init = 0.8 - 0.6 * float(np.exp(-0.3 * l))
        mod = (c_act @ ada_w[l] + ada_b[l]).reshape(B, N_MOD, D)
        shift1, scale1, gate1, shift2, scale2, gate2 = [mod[:, i, None, :] for i in range(N_MOD)]
        h = rms_norm(x, norm1_g[l]) * (1.0 + scale1) + shift1
        u = h @ w_in[l]
        (g_q, g_k, g_v, g_r, g_lr, d_q, d_k, d_v, gate_a, gate_b) = jnp.split(u, split_idx, axis=-1)
        o_a = gla_branch(g_q, g_k, g_v, g_r, g_lr, gla_alpha_up[l], gla_alpha_b[l], gla_out_g[l])
        o_b = diff_branch(d_q, d_k, d_v, cos, sin, diff_q_g[l], diff_k_g[l], diff_lq1[l],
                          diff_lk1[l], diff_lq2[l], diff_lk2[l], diff_out_g[l], lambda_init)
        merged = (jax.nn.sigmoid(gate_a) * (o_a @ w_branch_a[l])
                  + jax.nn.sigmoid(gate_b) * (o_b @ w_branch_b[l]))
        x = x + gate1 * (merged @ w_out[l])
        h2 = rms_norm(x, norm2_g[l]) * (1.0 + scale2) + shift2
        y = hier_moe(h2, router_group_w[l], router_group_b[l], router_expert_w[l],
                     router_expert_b[l], expert_w1[l], expert_w3[l], expert_w2[l])
        x = x + gate2 * y
    return x


_drawn_inputs = setup_inputs


def setup_inputs(seed=0):
    import zlib

    import numpy as np

    out = dict(_drawn_inputs(seed))
    spreads = {}
    factors = {'norm1_g': 3.61,
     'gla_out_g': 28.446,
     'diff_q_g': 8.0,
     'diff_k_g': 8.0,
     'diff_lq1': 5.275,
     'diff_lk1': 8.0,
     'diff_lq2': 5.263,
     'diff_lk2': 6.476,
     'diff_out_g': 145.105,
     'router_group_b': 25.008,
     'router_expert_b': 35.544,
     'norm2_g': 8.0}
    for name, (base, spread) in spreads.items():
        noise = np.random.default_rng([zlib.crc32(name.encode()), seed]).standard_normal(out[name].shape)
        drawn = base * np.exp(spread * noise) if base else spread * noise
        out[name] = __import__('jax').numpy.asarray(drawn.astype(out[name].dtype))
    for name, factor in factors.items():
        out[name] = (out[name] * factor).astype(out[name].dtype)
    return out
```

```python
from contextlib import ExitStack

import numpy as np
import concourse.bass as bass
from concourse import mybir

ALU = mybir.AluOpType
ACT = mybir.ActivationFunctionType
AX = mybir.AxisListType
F32 = mybir.dt.float32
BF16 = mybir.dt.bfloat16
I32 = mybir.dt.int32
U32 = mybir.dt.uint32
ds = bass.ds

P = 128
T = 1024
D = 1024
NT = T // P
KT = D // P
NH = 4
DK = 64
DV = 128
HW = NH * DV
RANK = 16
CH = 64
TAU = 16.0
ROPE = 16
HALF = ROPE // 2
THETA = 500000.0
EPS = 1e-6
LAMBDA_INIT = 0.8 - 0.6 * float(np.exp(-0.3 * 0))
NEG = -1e30
NG, EPG = 4, 8
NE = NG * EPG
DE = 512
NR = NG + NE
MAXOV = (2 * T) // P - 1
NBLK = NE + MAXOV
PAD = 2 * P
O_GQK, O_GV, O_GR, O_GLR = 0, 512, 1024, 1536
O_DQ, O_DK, O_DV, O_GA, O_GB = 1552, 2064, 2576, 3088, 4112
INV_FREQ = [float(f) for f in
            (np.float32(THETA) ** (-np.arange(HALF, dtype=np.float32) / np.float32(HALF)))]
TWO_PI_HI = 6.28125
TWO_PI_LO = float(2 * np.pi - 6.28125)
PI = 3.14159

SEMS = """
small_ld fills_done consts_done mask0 adab_ld ada_ld0 ada_ld1 ada_ld2 ada_ld3 ada_done
cact_e cact_1 rows_tr rows_cols mod1_ps mod1_done rope_step rope_arg rope_sin
lam_p lam_e lam_done
x_ld0 x_ld1 x_sq x_sd x_rs x_norm x_tr h_evd h_eva
w_ld proj_mm proj_free
qk_sq qk_sum qk_sd qk_rs qk_scaled rope_in rope_prod rope_done
mods_ps mods_col gates_done qk_tr qT_done kT_done
head_staged scores_ready max_ready nmax_ready exp_done att_r att_nr att_a att_tr aT_done att_o att_o_done
ob_sq ob_sum ob_sd ob_rs ob_norm ob_tr obT_done
alr_ones glr_mm glr_done z_mm z_step g_done cum_mm dec_mm eb_done dec_done
gla_zero gla_dec gla_in gla_vcopy gla_tr gla_qkT gla_att gla_attS gla_sc gla_mid gla_out_state gla_o gla_o_done
oa_sq oa_sum oa_sd oa_rs oa_n1 oa_silu oa_norm oa_tr oaT_done
gw_ld0 gw_ld1 g_mm g_sig g_prod g_free
wout_ld xh_ld0 xh_ld1 ms_ready mo_mm mo_gated x1_ready x1_sq x1_sd x1_rs xn2_ready x1_st0 x1_st1 xn_st0 xn_st1 h2_tr h2_evd h2_eva rt_mm rt_done
rt_step rt_diff rt_exp rt_m rt_rank_mm rt_dest
pad_st slot_scat tab_ld
w13_ld0 w13_ld1 w2_ld0 w2_ld1 tig_ready tis_ready xg_ld0 xg_ld1 m_tr m_evd m_eva m1_mm m_silu m_hh m2_tr m_hhT m2_mm m_wt m_y sc_done0 sc_done1
ovf_ready
""".split()


N_SMALL = 23


def build(nc, io, out):
    with ExitStack() as ctx:
        def sb(name, shape, dt=F32):
            return ctx.enter_context(nc.sbuf_tensor(name, shape, dt))

        s = {n: ctx.enter_context(nc.semaphore(n)) for n in SEMS}
        ada_ld = [s["ada_ld0"], s["ada_ld1"], s["ada_ld2"], s["ada_ld3"]]
        x_ld, xh_ld = [s["x_ld0"], s["x_ld1"]], [s["xh_ld0"], s["xh_ld1"]]
        gw_ld, w13_ld, w2_ld, xg_ld = ([s["gw_ld0"], s["gw_ld1"]], [s["w13_ld0"], s["w13_ld1"]],
                                       [s["w2_ld0"], s["w2_ld1"]], [s["xg_ld0"], s["xg_ld1"]])
        sc_done = [s["sc_done0"], s["sc_done1"]]
        x1_st, xn_st = [s["x1_st0"], s["x1_st1"]], [s["xn_st0"], s["xn_st1"]]

        xn_rows = nc.dram_tensor("xn_rows", [T + PAD, D], F32, kind="Internal").ap()
        slot_tab = nc.dram_tensor("slot_tab", [NBLK * P, 2], I32, kind="Internal").ap()

        PS = ctx.enter_context(nc.psum_tensor("PS", [P, 8, 512], F32))

        def bank(b, n=1):
            return PS[:, b:b + n, :].rearrange("p b n -> p (b n)")

        R1 = sb("R1", [P, 12288])
        HT = sb("HT", [P, 8192])
        R2 = sb("R2", [P, 8192])
        R3 = sb("R3", [P, 8192])
        R4 = sb("R4", [P, 8192])
        WK = sb("WK", [P, 4096])

        ident = sb("ident", [P, P])
        identb = sb("identb", [P, P], BF16)
        causal_neg = sb("causal_neg", [P, P], BF16)
        tri = sb("tri", [P, P])
        blk = sb("blk", [P, P])
        suf = sb("suf", [P, P])
        onesf = sb("onesf", [P, P])
        iota_e = sb("iota_e", [P, NE])
        pos_e = sb("pos_e", [P, NE])
        thr = sb("thr", [P, MAXOV])
        thr128 = sb("thr128", [P, NT - 1])
        gcols = sb("gcols", [P, 20])
        gpre = sb("gpre", [P, 2, ROPE])
        lam = sb("lam", [P, 8])
        rbias = sb("rbias", [P, NR])
        wr = sb("wr", [P, KT, NR])
        pos = sb("pos", [P, NT], I32)
        posf = sb("posf", [P, NT])
        cact = sb("cact", [P, 4, KT])
        S1 = sb("S1", [P, KT])
        A1 = sb("A1", [P, KT])
        S2 = sb("S2", [P, KT])
        A2 = sb("A2", [P, KT])
        gate = sb("gate", [P, 2, D])
        stat = sb("stat", [P, 4, 2])
        att_mx = sb("att_mx", [P, 2, 2])
        att_nm = sb("att_nm", [P, 2, 2])
        att_sum = sb("att_sum", [P, 2, 2])
        att_rc = sb("att_rc", [P, 2, 3])
        sso = sb("sso", [P, 2, NT * NH])
        dec = sb("dec", [P, NT * 4])
        dcur = sb("dcur", [P, 2, 4])
        pack = sb("pack", [P, 2, NT, 2], I32)
        dest_i = sb("dest_i", [P, 2 * NT], I32)
        tig = sb("tig", [P, 2, 1], I32)
        tis = sb("tis", [P, 2, 1], I32)
        wt = sb("wt", [P, 2])
        ovf = sb("ovf", [P, MAXOV + 1], I32)

        def rt_tile(name, *shape):
            return sb(name, [P, *shape])

        gm, ids, gsum, p_top, m1, m2 = (rt_tile(n, NT)[:, :] for n in ("rt_gm", "rt_ids", "rt_gsum", "rt_ptop", "rt_m1", "rt_m2"))
        cnt, extra, ovb, delta, ovf_f = (R2[:, 3584 + 32 * j:3616 + 32 * j] for j in range(5))
        ovf_f = ovf_f[:, 0:MAXOV + 1]
        rt_d = rt_tile("rt_dm", 2, NT)
        wide = R2[:, 0:2048].rearrange("p (x t n) -> p x t n", x=8, t=NT)
        eq_e, oh1, oh2 = (wide[:, j] for j in range(3))
        eq_g, oh_g, rt_gd = (wide[:, 3 + j, :, 0:NG] for j in range(3))

        small_w = sb("small_w", [P, 384])
        aup = small_w[0:RANK + 1, 0:256]
        wlr = small_w[:, 256:384].rearrange("p (k n) -> p k n", k=KT)
        logits = small_w[:, 0:NT * NR].rearrange("p (t n) -> p t n", t=NT)
        tab_fill = R2[:, 6144:6144 + 2 * (NBLK + 1)].bitcast(I32).rearrange("p (b c) -> p b c", c=2)
        ang = R2[:, 6272:6528].rearrange("p (x n) -> p x n", x=4)
        iota_i = R2[:, 6592:6624].bitcast(I32)
        pos_i = R2[:, 6624:6656].bitcast(I32)
        onesb = R4[:, 7168:7232].bitcast(BF16)
        before = R4[:, 7232:7296].bitcast(BF16)
        angi = R2[:, 6528:6592].bitcast(I32)
        lq = R2[:, 6656:6912].rearrange("p (x n) -> p x n", x=4)
        rows = R2[0:20, 6912:7040]
        sincos = R2[:, 7040:7168].rearrange("p (x t f) -> p x t f", x=2, t=NT)
        ssqk = WK[:, 768:896]
        rqk = WK[:, 896:1024].rearrange("p (t c) -> p t c", t=NT)
        tab = R2[:, 7680:7680 + 2 * NBLK].bitcast(I32).rearrange("p (b c) -> p b c", c=2)
        choice_b = R2[:, 3072:3072 + (2 * NT + 1) * NE // 2].bitcast(BF16).rearrange("p (t n) -> p t n", n=NE)
        U = R1[:, :].rearrange("p (t n) -> p t n", t=NT)
        hT = HT[:, :].rearrange("p (k t) -> p k t", k=KT)
        acc = R2[:, 0:6144].rearrange("p (g n) -> p g n", g=3)
        aw = [R4[:, 2048 * i:2048 * (i + 1)] for i in range(4)]
        wring = R3[:, :].rearrange("p (r k n) -> p r k n", r=2, k=KT)
        xb = [WK[:, 1024 * i:1024 * (i + 1)] for i in range(2)]
        ropeb = WK[:, 0:768]
        junk = [WK[:, 2048 + 1024 * i:2048 + 1024 * (i + 1)] for i in range(2)]
        qT = R2[:, 0:4096].rearrange("p (h t) -> p h t", h=NH)
        kT = R2[:, 4096:8192].rearrange("p (h t) -> p h t", h=NH)
        qs, ks = R4[:, 0:1024], R4[:, 1024:2048]
        E = R4[:, 2048:6144].rearrange("p (u c n) -> p u c n", u=2, c=2)
        attn = [R4[:, 6144 + 1024 * i:6144 + 1024 * (i + 1)] for i in range(2)]
        attnT = [WK[:, 1024 * i:1024 * (i + 1)] for i in range(2)]
        oaT = R4[:, 0:4096].rearrange("p (h t) -> p h t", h=NH)
        obT = R4[:, 4096:8192].rearrange("p (h t) -> p h t", h=NH)
        alrT = R4[0:RANK + 1, 0:1024]
        sp = R4[:, 1024:3072]
        G, EB, ENB, EKD = (R2[:, 2048 * i:2048 * (i + 1)].rearrange("p (t n) -> p t n", t=NT)
                           for i in range(4))
        gl = [WK[:, 0:2304], R4[:, 0:2304]]
        qin, kin, kdc, vcp = ([g[:, 0:256] for g in gl], [g[:, 256:512] for g in gl],
                              [g[:, 512:768] for g in gl], [g[:, 768:1280] for g in gl])
        qkT = [g[:, 1280:1792].rearrange("p (x t) -> p x t", x=4) for g in gl]
        attS = [g[:, 1792:2304].rearrange("p (h t) -> p h t", h=4) for g in gl]
        S_in = [R4[:, 2304 + 256 * i:2560 + 256 * i].rearrange("p (h v) -> p h v", h=2) for i in range(2)]
        S_mid = [R4[:, 2816 + 256 * i:3072 + 256 * i].rearrange("p (h v) -> p h v", h=2) for i in range(2)]
        gw = [R3[:, 3072 * i:3072 * (i + 1)].rearrange("p (k n) -> p k n", k=24) for i in range(2)]
        sig = R3[:, 6144:8192].rearrange("p (x n) -> p x n", x=4)
        mT = R2[:, :].rearrange("p (k t) -> p k t", k=KT)
        wout = R1[:, 0:8192].rearrange("p (k n) -> p k n", k=KT)
        xh = [R4[:, 4096 + 1024 * i:5120 + 1024 * i] for i in range(2)]
        ms = [R4[:, 6144 + 1024 * i:7168 + 1024 * i].rearrange("p (k t) -> p k t", k=KT) for i in range(2)]
        xn = [WK[:, 1024 * i:1024 * (i + 1)] for i in range(2)]
        h2T = [WK[:, 2048 + 1024 * i:3072 + 1024 * i].rearrange("p (k t) -> p k t", k=KT) for i in range(2)]
        earlier = R4[:, 6144:7168].rearrange("p (x y) -> p x y", y=NE)
        w13 = [HT[:, :].rearrange("p (w k n) -> p w k n", w=2, k=KT),
               R3[:, :].rearrange("p (w k n) -> p w k n", w=2, k=KT)]
        w2b = [R1[:, 8192:12288].rearrange("p (k n) -> p k n", k=4),
               R4[:, 0:4096].rearrange("p (k n) -> p k n", k=4)]
        xg = [R2[:, 1024 * i:1024 * (i + 1)] for i in range(2)]
        xT = [R2[:, 2048 + 1024 * i:3072 + 1024 * i].rearrange("p (k t) -> p k t", k=KT) for i in range(2)]
        yb = [R2[:, 4096 + 1024 * i:5120 + 1024 * i] for i in range(2)]
        sg, hh = R2[:, 6144:6656], R2[:, 6656:7168]
        hhT = R2[:, 7168:7680].rearrange("p (k t) -> p k t", k=4)
        zrow = R2[:, 7168:8192]

        w_in_v = io["w_in"].rearrange("(k p) n -> p k n", p=P)
        ada_v = io["ada_w"].rearrange("(p j) n -> p j n", j=KT)
        x_v = io["x"].rearrange("(t p) n -> t p n", p=P)
        out_v = out.rearrange("(t p) n -> t p n", p=P)
        xn_v = xn_rows.rearrange("(t p) n -> t p n", p=P)
        w1_v = io["expert_w1"].rearrange("e (k p) n -> e p k n", p=P)
        w3_v = io["expert_w3"].rearrange("e (k p) n -> e p k n", p=P)
        w2_v = io["expert_w2"].rearrange("e (k p) n -> e p k n", p=P)
        tab_v = slot_tab.rearrange("(b p) c -> p b c", p=P)

        def vec(name):
            return io[name].rearrange("(a n) -> a n", a=1)

        def wait_apart(e, *waits):
            values = [v if isinstance(v, int) else e.to_reg(v) for _, v in waits]
            e.wait_ge(s["consts_done"], 1)
            for (sem, _), v in zip(waits, values):
                e.wait_ge(sem, v)

        def expert_of(n):
            return (n % NG) * EPG + n // NG

        block = ctx.enter_context(nc.Block())

        @block.sync
        def _(sp_):
            e = sp_
            n_small = [0]

            def small(dst, src):
                n_small[0] += 1
                e.dma_start(dst, src, allow_slow_non_contiguous=True).then_inc(s["small_ld"], 16)

            e.wait_ge(s["fills_done"], 1)
            small(cact[:, 0, :], io["c"].rearrange("(p j) -> p j", j=KT))
            small(rows[0:8, :], io["norm1_g"].rearrange("(k p) -> k p", p=P))
            small(rows[8:16, :], io["norm2_g"].rearrange("(k p) -> k p", p=P))
            for r, nm in ((16, "diff_q_g"), (17, "diff_k_g")):
                for c in range(2):
                    small(rows[r:r + 1, c * DK + ROPE:(c + 1) * DK], vec(nm)[:, ROPE:DK])
            small(rows[18:19, :], vec("gla_out_g"))
            small(rows[19:20, :], vec("diff_out_g"))
            small(pos[:, :], io["positions"].rearrange("(t p) -> p t", p=P))
            small(gpre[:, 0, :], io["diff_q_g"][0:ROPE].partition_broadcast(P))
            small(gpre[:, 1, :], io["diff_k_g"][0:ROPE].partition_broadcast(P))
            for j, nm in enumerate(("diff_lq1", "diff_lk1", "diff_lq2", "diff_lk2")):
                small(lq[:, j, :], io[nm].partition_broadcast(P))
            small(rbias[:, 0:NG], io["router_group_b"].partition_broadcast(P))
            small(rbias[:, NG:NR], io["router_expert_b"].partition_broadcast(P))
            small(wr[:, :, 0:NG], io["router_group_w"].rearrange("(k p) n -> p k n", p=P))
            small(wr[:, :, NG:NR], io["router_expert_w"].rearrange("(k p) n -> p k n", p=P))
            small(aup[0:RANK, :], io["gla_alpha_up"])
            small(aup[RANK:RANK + 1, :], vec("gla_alpha_b"))
            small(wlr, w_in_v[:, :, O_GLR:O_GLR + RANK])
            assert n_small[0] == N_SMALL
            e.wait_ge(s["fills_done"], 2)
            e.dma_start(acc[0:1, :, :], vec("ada_b").rearrange("a (g n) -> a g n", g=3)).then_inc(s["adab_ld"], 16)

            def load_ada(g, j, dynamic):
                if dynamic or g * KT + j >= 4:
                    e.wait_ge(s["ada_done"], g * KT + j - 3)
                e.dma_start(aw[j % 4], ada_v[:, j, ds(g * 2048, 2048)]).then_inc(ada_ld[j % 4], 16)

            for j in range(KT):
                load_ada(0, j, False)
            for t in range(2):
                e.dma_start(xb[t], x_v[t]).then_inc(x_ld[t], 16)
            e.dma_start(wring[:, 0], w_in_v[:, :, O_DQ:O_DQ + HW]).then_inc(s["w_ld"], 16)
            with e.Fori(1, NT // 2) as i:
                for u in range(2):
                    e.wait_ge(s["x_tr"], 2 * i + u - 1)
                    e.dma_start(xb[u], x_v[2 * i + u]).then_inc(x_ld[u], 16)
            e.wait_ge(s["w_ld"], 16)
            e.dma_start(wring[:, 1], w_in_v[:, :, O_DK:O_DK + HW]).then_inc(s["w_ld"], 16)
            with e.Fori(1, 3) as g:
                for j in range(KT):
                    load_ada(g, j, True)
            e.wait_ge(s["consts_done"], 1)
            for u in range(2):
                e.dma_start(out_v[NT + u], zrow).then_inc(s["pad_st"], 16)
                e.dma_start(xn_v[NT + u], zrow).then_inc(s["pad_st"], 16)
            e.dma_start(tab_v, tab_fill[:, 0:NBLK, :]).then_inc(s["pad_st"], 16)
            for n, off in ((2, O_DV), (3, O_GQK), (4, O_GV), (5, O_GR)):
                e.wait_ge(s["w_ld"], 16 * n)
                e.wait_ge(s["proj_mm"], NT * (n - 1))
                e.dma_start(wring[:, n % 2], w_in_v[:, :, off:off + HW]).then_inc(s["w_ld"], 16)
            e.wait_ge(s["w_ld"], 16 * 6)
            e.wait_ge(s["proj_mm"], NT * 6)
            with e.Fori(0, KT // 2) as i:
                for u in range(2):
                    f = 2 * i + u
                    e.wait_ge(s["g_free"], 2 * f + 2)
                    for k0, nk, src in ((0, 8, w_in_v[:, :, ds(O_GA + f * P, P)]),
                                        (8, 8, w_in_v[:, :, ds(O_GB + f * P, P)]),
                                        (16, 4, io["w_branch_a"].rearrange("(k p) n -> p k n", p=P)[:, :, ds(f * P, P)]),
                                        (20, 4, io["w_branch_b"].rearrange("(k p) n -> p k n", p=P)[:, :, ds(f * P, P)])):
                        e.dma_start(gw[u][:, k0:k0 + nk, :], src).then_inc(gw_ld[u], 16)
            e.wait_ge(s["oa_norm"], NT)
            e.wait_ge(s["oa_tr"], NT)
            e.dma_start(wout, io["w_out"].rearrange("(k p) n -> p k n", p=P)).then_inc(s["wout_ld"], 16)
            e.dma_start(w2b[0], w2_v[0]).then_inc(w2_ld[0], 16)
            e.wait_ge(s["g_mm"], 2 * KT)
            e.wait_ge(s["g_free"], 4 + 2 * KT)
            for u in range(2):
                e.dma_start(xh[u], x_v[u]).then_inc(xh_ld[u], 16)
            e.dma_start(w13[0][:, 0], w1_v[0]).then_inc(w13_ld[0], 16)
            e.dma_start(w13[0][:, 1], w3_v[0]).then_inc(w13_ld[0], 16)
            e.dma_start(w13[1][:, 0], w1_v[expert_of(1)]).then_inc(w13_ld[1], 16)
            e.dma_start(w13[1][:, 1], w3_v[expert_of(1)]).then_inc(w13_ld[1], 16)
            e.dma_start(w2b[1], w2_v[expert_of(1)]).then_inc(w2_ld[1], 16)

            def store_x(t, u):
                e.wait_ge(s["x1_ready"], t + 1)
                e.dma_start(out_v[t], xh[u]).then_inc(x1_st[u], 16)
                e.wait_ge(s["xn2_ready"], t + 1)
                e.dma_start(xn_v[t], xn[u]).then_inc(xn_st[u], 16)

            with e.Fori(0, NT // 2 - 1) as i:
                for u in range(2):
                    store_x(2 * i + u, u)
                    e.wait_ge(x1_st[u], 16 * (i + 1))
                    e.wait_ge(s["x1_sq"], 2 * i + u + 1)
                    e.dma_start(xh[u], x_v[2 * i + u + 2]).then_inc(xh_ld[u], 16)
            for u in range(2):
                store_x(NT - 2 + u, u)
            def load_w13(u, n, ex):
                e.wait_ge(s["m1_mm"], n - 1)
                e.dma_start(w13[u][:, 0], w1_v[ex]).then_inc(w13_ld[u], 16)
                e.dma_start(w13[u][:, 1], w3_v[ex]).then_inc(w13_ld[u], 16)

            def load_w2(u, n, ex):
                e.wait_ge(s["m2_mm"], n)
                e.dma_start(w2b[u], w2_v[ex]).then_inc(w2_ld[u], 16)

            for n in (2, 3):
                load_w13(n % 2, n, expert_of(n))
                load_w2(n % 2, n, expert_of(n))
            with e.Fori(1, EPG) as i:
                for g in range(NG):
                    load_w13(g % 2, NG * i + g, EPG * g + i)
                    load_w2(g % 2, NG * i + g, EPG * g + i)
            e.wait_ge(s["ovf_ready"], 1)
            n_ov = e.value_load(ovf[0:1, MAXOV:MAXOV + 1], min_val=0, max_val=MAXOV)
            with e.If(n_ov > 0):
                with e.Fori(0, n_ov) as j:
                    ex = e.value_load(ovf[0:1, ds(j, 1)], min_val=0, max_val=NE - 1)
                    e.wait_ge(s["m2_mm"], NE + j + 1)
                    e.dma_start(w13[0][:, 0], w1_v[ex]).then_inc(w13_ld[0], 16)
                    e.dma_start(w13[0][:, 1], w3_v[ex]).then_inc(w13_ld[0], 16)
                    e.dma_start(w2b[0], w2_v[ex]).then_inc(w2_ld[0], 16)
            for u in range(2):
                e.wait_ge(x1_st[u], 16 * NT // 2)
                e.wait_ge(xn_st[u], 16 + 16 * NT // 2)
            e.wait_ge(s["pad_st"], 80)

        @block.gpsimd
        def _(e):
            e.memset(rows, 1.0)
            e.memset(aup, 0.0).then_inc(s["fills_done"], 1)
            e.memset(R2[:, 0:6144], 0.0).then_inc(s["fills_done"], 1)
            e.memset(zrow, 0.0)
            e.memset(ident[:, :], 0.0)
            e.memset(causal_neg[:, :], 0.0)
            e.memset(tri[:, :], 1.0 / TAU)
            e.memset(blk[:, :], 0.0)
            e.memset(onesf[:, :], 1.0)
            e.memset(tab_fill, 0)
            e.iota(pos_i, pattern=[[1, NG], [NG, EPG]], base=0, channel_multiplier=0)
            e.iota(iota_i, pattern=[[1, NE]], base=0, channel_multiplier=0).then_inc(s["mask0"], 1)
            e.wait_ge(s["mask0"], 1)
            e.affine_select(out=ident[:, :], in_=ident[:, :], compare_op=ALU.not_equal, fill=1.0,
                            base=0, pattern=[[-1, P]], channel_multiplier=1)
            e.affine_select(out=causal_neg[:, :], in_=causal_neg[:, :], compare_op=ALU.is_ge, fill=NEG,
                            base=0, pattern=[[-1, P]], channel_multiplier=1)
            e.affine_select(out=tri[:, :], in_=tri[:, :], compare_op=ALU.is_ge, fill=0.0,
                            base=0, pattern=[[1, P]], channel_multiplier=-1)
            e.iota(tab_fill[:, :, 0:1].rearrange("p (b u) c -> p b u c", u=2), pattern=[[0, (NBLK + 1) // 2], [P, 2], [0, 1]],
                   base=T, channel_multiplier=1)
            for k in range(2):
                e.iota(pack[:, k, :, 0:1], pattern=[[P, NT], [0, 1]], base=0, channel_multiplier=1)
            for n in range(NT - 1):
                e.memset(thr128[:, n:n + 1], float(P * (n + 1)))
            e.tensor_copy(iota_e[:, :], iota_i)
            e.tensor_copy(pos_e[:, :], pos_i)
            e.tensor_copy(thr[:, :], iota_i[:, 0:MAXOV]).then_inc(s["mask0"], 1)
            e.wait_ge(s["mask0"], 2)
            e.memset(tri[0:CH, CH:P], 0.0)
            e.memset(blk[0:CH, 0:CH], 1.0 / TAU)
            e.tensor_copy(identb[:, :], ident[:, :]).then_inc(s["mask0"], 1)
            e.wait_ge(s["mask0"], 3)
            e.memset(blk[CH:P, CH:P], 1.0 / TAU).then_inc(s["mask0"], 1)
            e.wait_ge(s["mask0"], 4)
            e.tensor_sub(suf[:, :], blk[:, :], tri[:, :]).then_inc(s["consts_done"], 1)

            e.wait_ge(s["qT_done"], NT)
            e.wait_ge(s["kT_done"], NT)
            with e.Fori(0, NH) as h:
                wait_apart(e, (s["scores_ready"], h * NT + 1))
                e.tensor_copy(qs, qT[:, h, :])
                e.tensor_copy(ks, kT[:, h, :]).then_inc(s["head_staged"], 1)

            e.wait_ge(s["att_o_done"], 2 + NH * NT)
            e.memset(R4[0:32, 0:1024], 1.0).then_inc(s["alr_ones"], 1)

            e.wait_ge(s["g_done"], 1)
            e.wait_ge(s["z_mm"], 1)
            e.wait_ge(s["obT_done"], NT)
            e.memset(attS[0], 0.0)
            e.memset(attS[1], 0.0)
            e.memset(S_in[0], 0.0).then_inc(s["gla_zero"], 1)
            e.wait_ge(s["proj_free"], 4 + 5 * NT)
            with e.Fori(0, NT // 2) as i:
                for u in range(2):
                    t = 2 * i + u
                    wait_apart(e, (s["gla_o"], t + 1))
                    e.tensor_copy(vcp[u], U[:, t, 1024:1536]).then_inc(s["gla_vcopy"], 1)

            e.wait_ge(s["g_free"], 4 + 2 * KT)
            with e.Fori(0, NT // 2) as i:
                for u in range(2):
                    t = 2 * i + u
                    wait_apart(e, (s["mo_mm"], t + 1))
                    e.tensor_copy(ms[u], mT[:, :, ds(t * P, P)]).then_inc(s["ms_ready"], 1)

            e.wait_ge(s["mo_mm"], 2 + NT)
            e.memset(onesb, 1.0)
            e.memset(before, 1.0)
            e.memset(earlier, 1.0).then_inc(s["mask0"], 1)
            e.wait_ge(s["mask0"], 5)
            e.affine_select(out=before, in_=before, compare_op=ALU.is_gt, fill=0.0,
                            base=0, pattern=[[1, P]], channel_multiplier=-1)
            e.affine_select(out=earlier, in_=earlier, compare_op=ALU.is_gt, fill=0.0,
                            base=0, pattern=[[1, NE], [-1, NE]], channel_multiplier=0).then_inc(s["mask0"], 1)

            e.wait_ge(s["rt_dest"], 1)
            e.wait_ge(s["pad_st"], 80)
            pk = pack[:, :, :, :].rearrange("p k t c -> p (k t) c")
            for n in range(2 * NT):
                e.indirect_dma_start(slot_tab, bass.IndirectOffsetOnAxis(dest_i[:, n:n + 1], 0),
                                     pk[:, n, :], None).then_inc(s["slot_scat"], 16)
            e.wait_ge(s["slot_scat"], 16 * 2 * NT)
            e.dma_start(tab, tab_v).then_inc(s["tab_ld"], 16)
            e.wait_ge(s["tab_ld"], 16)
            for u in range(2):
                e.wait_ge(x1_st[u], 16 * NT // 2)
                e.wait_ge(xn_st[u], 16 + 16 * NT // 2)
            e.wait_ge(s["pad_st"], 80)

            def gather(n, u):
                wait_apart(e, (s["m_tr"], n + 1))
                e.tensor_copy(tig[:, u, :], tab[:, ds(n, 1), 0:1].rearrange("p b c -> p (b c)")).then_inc(s["tig_ready"], 1)
                wait_apart(e, (s["tig_ready"], n + 1))
                e.indirect_dma_start(xg[u], None, xn_rows,
                                     bass.IndirectOffsetOnAxis(tig[:, u, :], 0)).then_inc(xg_ld[u], 16)

            def scatter(n, u, k):
                if not isinstance(k, int) or k > 0:
                    wait_apart(e, (sc_done[u], 16 * k))
                e.tensor_copy(tis[:, u, :], tab[:, ds(n, 1), 0:1].rearrange("p b c -> p (b c)")).then_inc(s["tis_ready"], 1)
                wait_apart(e, (s["tis_ready"], n + 1), (s["m_y"], n + 2))
                e.indirect_dma_start(out, bass.IndirectOffsetOnAxis(tis[:, u, :], 0), yb[u], None,
                                     compute_op=ALU.add).then_inc(sc_done[u], 16)

            for n in range(4):
                gather(n, n % 2)
            for n in range(2):
                gather(n + 4, n)
                scatter(n, n, 0)
            with e.Fori(1, NE // 2 - 2) as i:
                for u in range(2):
                    gather(2 * i + u + 4, u)
                    scatter(2 * i + u, u, i)
            for n in range(NE - 4, NE):
                scatter(n, n % 2, n // 2)
            for u in range(2):
                e.wait_ge(sc_done[u], 16 * NE // 2)
            e.wait_ge(s["ovf_ready"], 1)
            n_ov = e.value_load(ovf[0:1, MAXOV:MAXOV + 1], min_val=0, max_val=MAXOV)
            with e.If(n_ov > 0):
                with e.Fori(0, n_ov) as j:
                    gather(NE + j, 0)
                    scatter(NE + j, 0, NE // 2 + j)
                    wait_apart(e, (sc_done[0], 16 * (NE // 2 + j + 1)))

        @block.tensor
        def _(e):
            def mm(o, l, r, a=True, z=True):
                return nc.tensor.matmul(o, l, r, start=a, stop=z)

            e.wait_ge(s["small_ld"], 16 * N_SMALL)
            e.wait_ge(s["consts_done"], 1)
            nc.tensor.transpose(bank(0)[:, 0:20], rows, ident[0:20, 0:20]).then_inc(s["rows_tr"], 1)
            e.wait_ge(s["ada_done"], KT)
            for j in range(2 * KT):
                last = mm(bank(1)[:, j:j + 1], acc[:, 0, j * P:(j + 1) * P], onesf[:, 0:1])
            last.then_inc(s["mod1_ps"], 1)

            with e.Fori(0, NT // 2) as i:
                for u in range(2):
                    t = 2 * i + u
                    e.wait_ge(s["x_norm"], t + 1)
                    e.wait_ge(s["h_evd"], t + 1)
                    e.wait_ge(s["h_eva"], t + 1)
                    for k in range(KT):
                        last = nc.tensor.transpose(bank(4 + 2 * u + k // 4)[:, (k % 4) * P:(k % 4 + 1) * P],
                                                   xb[u][:, k * P:(k + 1) * P], ident[:, :])
                    last.then_inc(s["x_tr"], 1)
            e.wait_ge(s["h_evd"], 2 + NT)
            e.wait_ge(s["h_eva"], 2 + NT)

            def project(n):
                e.wait_ge(s["w_ld"], 16 * (n + 1))
                for t in range(NT):
                    e.wait_ge(s["proj_free"], n * NT + t + 1)
                    for k in range(KT):
                        last = mm(bank(t % 4), hT[:, k, t * P:(t + 1) * P], wring[:, n % 2, k, :],
                                  k == 0, k == KT - 1)
                    last.then_inc(s["proj_mm"], 1)

            with e.Fori(0, 3) as n:
                project(n)

            e.wait_ge(s["ada_done"], 3 * KT)
            e.wait_ge(s["proj_free"], 4 + 3 * NT)
            for j in range(KT):
                mm(bank(0)[:, j:j + 1], acc[:, 1, 1024 + j * P:1024 + (j + 1) * P], onesf[:, 0:1])
            for j in range(KT):
                mm(bank(0)[:, 8 + j:9 + j], acc[:, 2, j * P:(j + 1) * P], onesf[:, 0:1])
            for b, (g, o) in enumerate(((1, 0), (1, 512), (2, 1024), (2, 1536))):
                last = mm(bank(4 + b), onesf[:, :], acc[:, g, o:o + 512])
            last.then_inc(s["mods_ps"], 1)

            e.wait_ge(s["gates_done"], 1)
            for t in range(NT):
                e.wait_ge(s["rope_done"], t + 1)
                if t >= 2:
                    e.wait_ge(s["qT_done"], t - 1)
                    e.wait_ge(s["kT_done"], t - 1)
                for h in range(2 * NH):
                    last = nc.tensor.transpose(bank(4 + 2 * (t % 2) + h // NH)[:, (h % NH) * P:(h % NH + 1) * P],
                                               U[:, t, h * P:(h + 1) * P], ident[:, :])
                last.then_inc(s["qk_tr"], 1)
            e.wait_ge(s["mods_col"], 1)

            with e.Fori(0, NH) as h:
                def scores(i):
                    if i == 0:
                        e.wait_ge(s["head_staged"], h + 1)
                    e.wait_ge(s["exp_done"], h * NT + i + 1)
                    n = (i + 1) * P
                    for b in range((n + 511) // 512):
                        w = min(512, n - 512 * b)
                        diag = 512 * b + w == n
                        for c in range(2):
                            mm(bank(2 * c + b)[:, 0:w], qs[c * DK:(c + 1) * DK, i * P:(i + 1) * P],
                               ks[c * DK:(c + 1) * DK, 512 * b:512 * b + w], True, not diag)
                    for c in range(2):
                        last = mm(bank(2 * c + i // 4)[:, (i % 4) * P:(i % 4 + 1) * P],
                                  identb[:, :], causal_neg[:, :], False, True)
                    last.then_inc(s["scores_ready"], 1)

                def turn(i):
                    e.wait_ge(s["att_a"], h * NT + i + 3)
                    e.wait_ge(s["aT_done"], h * NT + i + 1)
                    for j in range(i + 1):
                        last = nc.tensor.transpose(bank(4 + j // 4)[:, (j % 4) * P:(j % 4 + 1) * P],
                                                   attn[i % 2][:, j * P:(j + 1) * P], ident[:, :])
                    last.then_inc(s["att_tr"], 1)

                def weigh(i):
                    e.wait_ge(s["aT_done"], h * NT + i + 2)
                    e.wait_ge(s["att_o_done"], h * NT + i + 1)
                    for j in range(i + 1):
                        last = mm(bank(6 + i % 2)[:, 0:DV], attnT[i % 2][:, j * P:(j + 1) * P],
                                  U[:, j, ds(1024 + h * DV, DV)], j == 0, j == i)
                    last.then_inc(s["att_o"], 1)

                scores(0)
                for i in range(NT):
                    if i + 1 < NT:
                        scores(i + 1)
                    turn(i)
                    if i >= 1:
                        weigh(i - 1)
                weigh(NT - 1)

            with e.Fori(3, 5) as n:
                project(n)
            for t in range(NT):
                e.wait_ge(s["ob_norm"], t + 1)
                if t >= 2:
                    e.wait_ge(s["obT_done"], t - 1)
                for h in range(NH):
                    last = nc.tensor.transpose(bank(4 + t % 2)[:, h * P:(h + 1) * P],
                                               U[:, t, h * P:(h + 1) * P], ident[:, :])
                last.then_inc(s["ob_tr"], 1)
            project(5)
            for half in range(2):
                for k in range(KT):
                    last = mm(bank(6 + half)[0:RANK, :], wlr[:, k, :], hT[:, k, half * 512:(half + 1) * 512],
                              k == 0, k == KT - 1)
            last.then_inc(s["glr_mm"], 1)
            e.wait_ge(s["glr_done"], 1)
            e.wait_ge(s["proj_free"], 4 + 6 * NT)
            for t in range(NT):
                last = mm(bank(0, 4)[:, t * 256:(t + 1) * 256], alrT[:, t * P:(t + 1) * P], aup)
            last.then_inc(s["z_mm"], 1)
            e.wait_ge(s["g_done"], 1)
            e.wait_ge(s["obT_done"], NT)
            for b in range(4):
                mm(bank(b), tri[:, :], R2[:, 512 * b:512 * (b + 1)])
            for b in range(4):
                last = mm(bank(4 + b), suf[:, :], R2[:, 512 * b:512 * (b + 1)])
            last.then_inc(s["cum_mm"], 1)
            e.wait_ge(s["eb_done"], 1)
            for t in range(NT):
                for pr in range(2):
                    last = mm(bank(7)[:, t * 4 + pr * 2:t * 4 + pr * 2 + 2],
                              R2[:, t * 256 + pr * P:t * 256 + (pr + 1) * P], blk[:, 0:P:CH])
            last.then_inc(s["dec_mm"], 1)

            def gla_o(t, u):
                e.wait_ge(s["gla_attS"], t + 1)
                e.wait_ge(s["gla_mid"], t + 1)
                e.wait_ge(s["gla_o_done"], t + 1)
                for hd in range(NH):
                    r0, pr = DK * (hd % 2), hd // 2
                    o = bank(5 + hd % 2)[:, pr * DV:(pr + 1) * DV]
                    mm(o, attS[u][:, hd, :], vcp[u][:, hd * DV:(hd + 1) * DV], True, False)
                    mm(o[0:CH, :], qkT[u][r0:r0 + DK, pr, 0:CH], S_in[u][r0:r0 + DK, pr, :], False, True)
                    last = mm(o[CH:P, :], qkT[u][r0:r0 + DK, pr, CH:P], S_mid[u][r0:r0 + DK, pr, :], False, True)
                last.then_inc(s["gla_o"], 1)

            def gla_first(t, u):
                e.wait_ge(s["gla_in"], t + 1)
                e.wait_ge(s["gla_qkT"], t + 1)
                for x in range(4):
                    src = (qin, kin)[x // 2][u][:, (x % 2) * P:(x % 2 + 1) * P]
                    last = nc.tensor.transpose(bank(0)[:, x * P:(x + 1) * P], src, ident[:, :])
                last.then_inc(s["gla_tr"], 1)
                wait_apart(e, (s["gla_vcopy"], t + 1), (s["gla_out_state"], t + 1))
                for c in range(2):
                    for hd in range(NH):
                        r0, pr = DK * (hd % 2), hd // 2
                        last = mm(bank(3 + c)[r0:r0 + DK, pr * DV:(pr + 1) * DV],
                                  kdc[u][c * CH:(c + 1) * CH, hd * DK:(hd + 1) * DK],
                                  vcp[u][c * CH:(c + 1) * CH, hd * DV:(hd + 1) * DV])
                last.then_inc(s["gla_sc"], 1)

            def gla_att(t, u):
                e.wait_ge(s["gla_qkT"], t + 2)
                for hd in range(NH):
                    r0, pr = DK * (hd % 2), hd // 2
                    last = mm(bank(1 + hd % 2)[:, pr * P:(pr + 1) * P], qkT[u][r0:r0 + DK, 2 + pr, :],
                              qkT[u][r0:r0 + DK, pr, :])
                last.then_inc(s["gla_att"], 1)

            e.wait_ge(s["dec_done"], 1)
            e.wait_ge(s["gla_zero"], 1)
            gla_first(0, 0)
            gla_att(0, 0)
            with e.Fori(0, NT // 2 - 1) as i:
                for u in range(2):
                    t = 2 * i + u
                    gla_first(t + 1, 1 - u)
                    gla_o(t, u)
                    gla_att(t + 1, 1 - u)
            gla_first(NT - 1, 1)
            gla_o(NT - 2, 0)
            gla_att(NT - 1, 1)
            gla_o(NT - 1, 1)

            for t in range(NT):
                e.wait_ge(s["oa_norm"], t + 1)
                if t == 0:
                    e.wait_ge(s["gla_o_done"], 1 + NT)
                if t >= 2:
                    e.wait_ge(s["oaT_done"], t - 1)
                for h in range(NH):
                    last = nc.tensor.transpose(bank(t % 2)[:, h * P:(h + 1) * P],
                                               U[:, t, 1024 + h * P:1024 + (h + 1) * P], ident[:, :])
                last.then_inc(s["oa_tr"], 1)
            e.wait_ge(s["oaT_done"], NT)

            with e.Fori(0, KT // 2) as i:
                for u in range(2):
                    e.wait_ge(gw_ld[u], 64 * (i + 1))
                    for half in range(2):
                        e.wait_ge(s["g_free"], 2 * (2 * i + u) + half + 3)
                        tok = slice(half * 512, (half + 1) * 512)
                        for b, (k0, nk, src) in enumerate(((0, 8, hT), (8, 8, hT), (16, 4, oaT), (20, 4, obT))):
                            for k in range(nk):
                                last = mm(bank(4 * half + b), gw[u][:, k0 + k, :], src[:, k, tok],
                                          k == 0, k == nk - 1)
                        last.then_inc(s["g_mm"], 1)

            e.wait_ge(s["wout_ld"], 16)
            e.wait_ge(s["g_free"], 4 + 2 * KT)

            def out_proj(t, u):
                e.wait_ge(s["ms_ready"], t + 1)
                e.wait_ge(s["mo_gated"], t + 1)
                for half in range(2):
                    for k in range(KT):
                        last = mm(bank(2 * u + half), ms[u][:, k, :], wout[:, k, half * 512:(half + 1) * 512],
                                  k == 0, k == KT - 1)
                last.then_inc(s["mo_mm"], 1)

            def turn_h2(t, u):
                e.wait_ge(s["xn2_ready"], t + 1)
                e.wait_ge(s["h2_evd"], t + 1)
                e.wait_ge(s["h2_eva"], t + 1)
                for k in range(KT):
                    last = nc.tensor.transpose(bank(4 + k // 4)[:, (k % 4) * P:(k % 4 + 1) * P],
                                               xn[u][:, k * P:(k + 1) * P], ident[:, :])
                last.then_inc(s["h2_tr"], 1)

            def route(t, u):
                e.wait_ge(s["h2_evd"], t + 2)
                e.wait_ge(s["h2_eva"], t + 2)
                e.wait_ge(s["rt_done"], t + 1)
                for k in range(KT):
                    last = mm(bank(6)[:, 0:NR], h2T[u][:, k, :], wr[:, k, :], k == 0, k == KT - 1)
                last.then_inc(s["rt_mm"], 1)

            out_proj(0, 0)
            with e.Fori(0, NT // 2 - 1) as i:
                for u in range(2):
                    t = 2 * i + u
                    out_proj(t + 1, 1 - u)
                    turn_h2(t, u)
                    route(t, u)
            out_proj(NT - 1, 1)
            for t in (NT - 2, NT - 1):
                turn_h2(t, t % 2)
                route(t, t % 2)

            e.wait_ge(s["rt_m"], 1)
            e.wait_ge(s["mask0"], 6)
            mm(bank(0)[:, 0:NT * NE], before, choice_b[:, 0:NT, :].rearrange("p t e -> p (t e)"), True, False)
            mm(bank(0)[:, 0:NT * NE], onesb, choice_b[:, NT:2 * NT, :].rearrange("p t e -> p (t e)"), False, True)
            mm(bank(1)[:, 0:NE], onesb, choice_b[:, 2 * NT, :]).then_inc(s["rt_rank_mm"], 1)

            def rows_in(n, u, k):
                e.wait_ge(xg_ld[u], 16 * (k + 1))
                e.wait_ge(s["m_evd"], n + 1)
                e.wait_ge(s["m_eva"], n + 1)
                for j in range(KT):
                    last = nc.tensor.transpose(bank(j // 4)[:, (j % 4) * P:(j % 4 + 1) * P],
                                               xg[u][:, j * P:(j + 1) * P], ident[:, :])
                last.then_inc(s["m_tr"], 1)

            def up(n, u, k):
                e.wait_ge(s["m_evd"], n + 2)
                e.wait_ge(s["m_eva"], n + 2)
                e.wait_ge(w13_ld[u], 32 * (k + 1))
                e.wait_ge(s["m_hh"], n + 1)
                for w in range(2):
                    for j in range(KT):
                        last = mm(bank(2 + w), xT[u][:, j, :], w13[u][:, w, j, :], j == 0, j == KT - 1)
                last.then_inc(s["m1_mm"], 1)

            def turn_hh(n):
                e.wait_ge(s["m_hh"], n + 2)
                e.wait_ge(s["m_hhT"], n + 1)
                for j in range(4):
                    last = nc.tensor.transpose(bank(4)[:, j * P:(j + 1) * P], hh[:, j * P:(j + 1) * P], ident[:, :])
                last.then_inc(s["m2_tr"], 1)

            def down(n, u, k):
                e.wait_ge(s["m_hhT"], n + 2)
                e.wait_ge(w2_ld[u], 16 * (k + 1))
                e.wait_ge(s["m_y"], n + 1)
                for half in range(2):
                    for j in range(4):
                        last = mm(bank(6 + half), hhT[:, j, :], w2b[u][:, j, half * 512:(half + 1) * 512],
                                  j == 0, j == 3)
                last.then_inc(s["m2_mm"], 1)

            rows_in(0, 0, 0)
            up(0, 0, 0)
            rows_in(1, 1, 0)
            with e.Fori(0, NE // 2 - 1) as i:
                for u in (1, 0):
                    n = 2 * i + 2 - u
                    turn_hh(n - 1)
                    up(n, u, i + 1 - u)
                    rows_in(n + 1, 1 - u, i + 1)
                    down(n - 1, 1 - u, i)
            kl = NE // 2 - 1
            turn_hh(NE - 2)
            up(NE - 1, 1, kl)
            down(NE - 2, 0, kl)
            turn_hh(NE - 1)
            down(NE - 1, 1, kl)
            e.wait_ge(s["ovf_ready"], 1)
            n_ov = e.value_load(ovf[0:1, MAXOV:MAXOV + 1], min_val=0, max_val=MAXOV)
            with e.If(n_ov > 0):
                with e.Fori(0, n_ov) as j:
                    n, k = NE + j, NE // 2 + j
                    rows_in(n, 0, k)
                    up(n, 0, k)
                    turn_hh(n)
                    down(n, 0, k)

        @block.scalar
        def _(e):
            def act(o, i, f, **kw):
                return nc.scalar.activation(o, i, f, **kw)

            for sem, n in ((s["h_eva"], 2), (s["proj_free"], 4), (s["exp_done"], 1), (s["aT_done"], 1), (s["gla_qkT"], 1),
                           (s["gla_o_done"], 1), (s["h2_eva"], 1), (s["m_eva"], 1), (s["m_hhT"], 1), (s["scores_ready"], 1),
                           (s["m2_mm"], 1)):
                e.sem_inc(sem, n)
            e.wait_ge(s["small_ld"], 16 * N_SMALL)
            act(cact[:, 1, :], cact[:, 0, :], ACT.Exp, scale=-1.0).then_inc(s["cact_e"], 1)
            e.wait_ge(s["lam_p"], 1)
            act(lam[:, 2:4], lam[:, 0:2], ACT.Exp).then_inc(s["lam_e"], 1)
            e.wait_ge(s["rope_arg"], 1)
            act(sincos[:, 0].rearrange("p t f -> p (t f)"), ang[:, 3, :], ACT.Sin)
            act(sincos[:, 1].rearrange("p t f -> p (t f)"), ang[:, 2, :], ACT.Sin).then_inc(s["rope_sin"], 1)

            with e.Fori(0, NT // 2) as i:
                for u in range(2):
                    t = 2 * i + u
                    e.wait_ge(x_ld[u], 16 * (i + 1))
                    act(junk[u], xb[u], ACT.Square, accum_out=stat[:, 0, u:u + 1]).then_inc(s["x_sq"], 1)
                    e.wait_ge(s["x_sq"], t + 1)
                    act(stat[:, 1, u:u + 1], stat[:, 0, u:u + 1], ACT.Sqrt, scale=1.0 / D, bias=EPS).then_inc(s["x_sd"], 1)
                    e.wait_ge(s["mod1_done"], 1)
                    e.wait_ge(s["x_tr"], t + 1)
                    for k in range(4):
                        last = act(hT[:, 4 + k, ds(t * P, P)], bank(5 + 2 * u)[:, k * P:(k + 1) * P], ACT.Identity,
                                   scale=A1[:, 4 + k:5 + k], bias=S1[:, 4 + k:5 + k])
                    last.then_inc(s["h_eva"], 1)

            def read_section(n, col):
                for t in range(NT):
                    e.wait_ge(s["proj_mm"], n * NT + t + 1)
                    act(U[:, t, ds(col, HW)], bank(t % 4), ACT.Copy).then_inc(s["proj_free"], 1)

            with e.Fori(0, 2) as n:
                read_section(n, n * HW)
            with e.Fori(0, NT // 2) as i:
                for u in range(2):
                    t = 2 * i + u
                    e.wait_ge(s["proj_free"], 4 + NT + t + 1)
                    e.wait_ge(s["qk_sum"], t + 1)
                    act(junk[u], U[:, t, 0:1024], ACT.Square).then_inc(s["qk_sq"], 1)
            e.wait_ge(s["qk_sum"], 2 + NT)
            act(ssqk, ssqk, ACT.Sqrt, scale=1.0 / DK, bias=EPS).then_inc(s["qk_sd"], 1)
            read_section(2, 2 * HW)
            e.wait_ge(s["mods_ps"], 1)
            for b in range(4):
                last = act(gate[:, b // 2, (b % 2) * 512:(b % 2 + 1) * 512], bank(4 + b), ACT.Copy)
            last.then_inc(s["gates_done"], 1)
            for t in range(NT):
                e.wait_ge(s["qk_tr"], t + 1)
                act(qT[:, :, t * P:(t + 1) * P], bank(4 + 2 * (t % 2)).rearrange("p (h t) -> p h t", h=NH),
                    ACT.Copy, scale=gcols[:, 16:17]).then_inc(s["qT_done"], 1)

            with e.Fori(0, NH) as h:
                def exps(i):
                    e.wait_ge(s["nmax_ready"], h * NT + i + 1)
                    e.wait_ge(s["att_a"], h * NT + i + 1)
                    for c in range(2):
                        last = act(E[:, i % 2, c, 0:(i + 1) * P], bank(2 * c, 2)[:, 0:(i + 1) * P], ACT.Exp,
                                   scale=DK ** -0.5, bias=att_nm[:, i % 2, c:c + 1],
                                   accum_out=att_sum[:, i % 2, c:c + 1])
                    last.then_inc(s["exp_done"], 1)

                exps(0)
                for i in range(NT):
                    if i + 1 < NT:
                        exps(i + 1)
                    e.wait_ge(s["att_tr"], h * NT + i + 3)
                    e.wait_ge(s["att_o"], h * NT + i + 1)
                    act(attnT[i % 2][:, 0:(i + 1) * P], bank(4, 2)[:, 0:(i + 1) * P], ACT.Copy).then_inc(s["aT_done"], 1)

            def ob_square(t, u):
                e.wait_ge(s["ob_sum"], t + 1)
                act(junk[u][:, 0:HW], U[:, t, 0:HW], ACT.Square).then_inc(s["ob_sq"], 1)

            e.wait_ge(s["att_o_done"], 2 + NH * NT)
            with e.Fori(0, NT // 2) as i:
                for u in range(2):
                    ob_square(2 * i + u, u)
            e.wait_ge(s["ob_sum"], 2 + NT)
            act(sso[:, 0, :], sso[:, 0, :], ACT.Sqrt, scale=1.0 / DV, bias=EPS).then_inc(s["ob_sd"], 1)
            with e.Fori(3, 5) as n:
                read_section(n, (n - 2) * HW)
            for t in range(NT):
                e.wait_ge(s["ob_tr"], t + 1)
                act(obT[:, :, t * P:(t + 1) * P], bank(4 + t % 2).rearrange("p (h t) -> p h t", h=NH),
                    ACT.Copy, scale=gcols[:, 19:20]).then_inc(s["obT_done"], 1)
            read_section(5, 0)

            e.wait_ge(s["glr_mm"], 1)
            e.wait_ge(s["alr_ones"], 1)
            for half in range(2):
                last = act(R4[0:RANK, half * 512:(half + 1) * 512], bank(6 + half)[0:RANK, :], ACT.Copy)
            last.then_inc(s["glr_done"], 1)
            e.wait_ge(s["z_mm"], 1)
            act(sp, bank(0, 4), ACT.Abs).then_inc(s["z_step"], 1)
            e.wait_ge(s["z_step"], 1)
            act(sp, sp, ACT.Exp, scale=-1.0).then_inc(s["z_step"], 1)
            e.wait_ge(s["z_step"], 2)
            act(sp, sp, ACT.Ln, bias=1.0).then_inc(s["z_step"], 1)
            e.wait_ge(s["cum_mm"], 1)
            act(R2[:, 6144:8192], bank(4, 4), ACT.Exp).then_inc(s["eb_done"], 1)
            act(R2[:, 2048:4096], bank(0, 4), ACT.Exp).then_inc(s["eb_done"], 1)
            act(R2[:, 4096:6144], bank(0, 4), ACT.Exp, scale=-1.0).then_inc(s["eb_done"], 1)
            e.wait_ge(s["dec_mm"], 1)
            act(dec[:, :], bank(7)[:, 0:4 * NT], ACT.Exp).then_inc(s["dec_done"], 1)

            def gla_read(t, u):
                e.wait_ge(s["gla_tr"], t + 1)
                e.wait_ge(s["gla_o"], t + 1)
                act(qkT[u].rearrange("p x t -> p (x t)"), bank(0), ACT.Copy).then_inc(s["gla_qkT"], 1)

            def gla_out(t):
                e.wait_ge(s["gla_o"], t + 3)
                for par in range(2):
                    last = act(U[:, t, 1024:1536].rearrange("p (x y v) -> p x y v", x=2, y=2)[:, :, par, :],
                               bank(5 + par)[:, 0:256].rearrange("p (x v) -> p x v", x=2), ACT.Copy)
                last.then_inc(s["gla_o_done"], 1)

            gla_read(0, 0)
            with e.Fori(0, NT // 2 - 1) as i:
                for u in range(2):
                    gla_read(2 * i + u + 1, 1 - u)
                    gla_out(2 * i + u)
            gla_read(NT - 1, 1)
            gla_out(NT - 2)
            gla_out(NT - 1)

            e.wait_ge(s["gla_o_done"], 1 + NT)
            with e.Fori(0, NT // 2) as i:
                for u in range(2):
                    e.wait_ge(s["oa_sum"], 2 * i + u + 1)
                    act(junk[u][:, 0:HW], U[:, 2 * i + u, 1024:1536], ACT.Square).then_inc(s["oa_sq"], 1)
            e.wait_ge(s["oa_sum"], 2 + NT)
            act(sso[:, 1, :], sso[:, 1, :], ACT.Sqrt, scale=1.0 / DV, bias=EPS).then_inc(s["oa_sd"], 1)
            act(U[:, :, 0:HW], U[:, :, 0:HW], ACT.Silu).then_inc(s["oa_silu"], 1)
            for t in range(NT):
                e.wait_ge(s["oa_tr"], t + 1)
                act(oaT[:, :, t * P:(t + 1) * P], bank(t % 2).rearrange("p (h t) -> p h t", h=NH),
                    ACT.Copy, scale=gcols[:, 18:19]).then_inc(s["oaT_done"], 1)

            with e.Fori(0, 2 * KT, 2) as n:
                for half in range(2):
                    e.wait_ge(s["g_mm"], n + half + 1)
                    e.wait_ge(s["g_free"], n + half + 3)
                    act(sig[:, 2 * half, :], bank(4 * half), ACT.Sigmoid)
                    act(sig[:, 2 * half + 1, :], bank(4 * half + 1), ACT.Sigmoid).then_inc(s["g_sig"], 1)

            with e.Fori(0, NT // 2) as i:
                for u in range(2):
                    t = 2 * i + u
                    e.wait_ge(s["x1_ready"], t + 1)
                    e.wait_ge(s["rt_mm"], t + 1)
                    act(h2T[u].rearrange("p k t -> p (k t)"), xh[u], ACT.Square,
                        accum_out=stat[:, 2, u:u + 1]).then_inc(s["x1_sq"], 1)
                    e.wait_ge(s["x1_sq"], t + 1)
                    act(stat[:, 3, u:u + 1], stat[:, 2, u:u + 1], ACT.Sqrt, scale=1.0 / D, bias=EPS).then_inc(s["x1_sd"], 1)
                    e.wait_ge(s["x1_rs"], t + 1)
                    act(xn[u], xh[u], ACT.Copy, scale=stat[:, 2, u:u + 1]).then_inc(s["xn2_ready"], 1)
                    e.wait_ge(s["h2_tr"], t + 3)
                    for k in range(4):
                        last = act(h2T[u][:, 4 + k, :], bank(5)[:, k * P:(k + 1) * P], ACT.Identity,
                                   scale=A2[:, 4 + k:5 + k], bias=S2[:, 4 + k:5 + k])
                    last.then_inc(s["h2_eva"], 1)

            e.wait_ge(s["rt_diff"], 1)
            act(rt_gd, rt_gd, ACT.Exp).then_inc(s["rt_exp"], 1)
            e.wait_ge(s["rt_diff"], 2)
            act(rt_d[:, 1, :], rt_d[:, 0, :], ACT.Exp).then_inc(s["rt_exp"], 1)

            def rows_read(n, u):
                e.wait_ge(s["m_tr"], n + 3)
                for k in range(4):
                    last = act(xT[u][:, 4 + k, :], bank(1)[:, k * P:(k + 1) * P], ACT.Identity,
                               scale=A2[:, 4 + k:5 + k], bias=S2[:, 4 + k:5 + k])
                last.then_inc(s["m_eva"], 1)

            def silu(n):
                e.wait_ge(s["m1_mm"], n + 1)
                e.wait_ge(s["m_hh"], n + 1)
                act(sg, bank(2), ACT.Silu).then_inc(s["m_silu"], 1)

            def hh_read(n):
                e.wait_ge(s["m2_tr"], n + 2)
                e.wait_ge(s["m2_mm"], n + 1)
                act(hhT.rearrange("p k t -> p (k t)"), bank(4), ACT.Copy).then_inc(s["m_hhT"], 1)

            rows_read(0, 0)
            silu(0)
            rows_read(1, 1)
            with e.Fori(0, NE // 2 - 1) as i:
                for u in (1, 0):
                    n = 2 * i + 2 - u
                    hh_read(n - 1)
                    silu(n)
                    rows_read(n + 1, 1 - u)
            hh_read(NE - 2)
            silu(NE - 1)
            hh_read(NE - 1)
            e.wait_ge(s["ovf_ready"], 1)
            n_ov = e.value_load(ovf[0:1, MAXOV:MAXOV + 1], min_val=0, max_val=MAXOV)
            with e.If(n_ov > 0):
                with e.Fori(0, n_ov) as j:
                    rows_read(NE + j, 0)
                    silu(NE + j)
                    hh_read(NE + j)

        @block.vector
        def _(e):
            v = nc.vector

            def tt(o, a, b, op):
                return v.tensor_tensor(o, a, b, op)

            def tsc(o, a, c1, op0, c2=None, op1=None):
                if op1 is None:
                    return v.tensor_scalar(o, a, c1, None, op0)
                return v.tensor_scalar(o, a, c1, c2, op0, op1)

            def stt(o, a, c, b, op0, op1):
                return v.scalar_tensor_tensor(out=o, in0=a, scalar=c, in1=b, op0=op0, op1=op1)

            def spread(a, shape):
                return a.to_broadcast(shape)

            for sem, n in ((s["h_evd"], 2), (s["qk_sum"], 2), (s["att_a"], 2), (s["att_o"], 2), (s["att_tr"], 2), (s["att_o_done"], 2),
                           (s["ob_sum"], 2), (s["oa_sum"], 2), (s["gla_sc"], 2), (s["gla_o"], 2), (s["gla_out_state"], 1),
                           (s["g_free"], 4), (s["mo_mm"], 2), (s["mo_gated"], 2), (s["h2_tr"], 2), (s["h2_evd"], 1), (s["rt_mm"], 2),
                           (s["rt_done"], 1), (s["m_tr"], 2), (s["m_evd"], 1), (s["m_hh"], 1), (s["m2_tr"], 1),
                           (s["m_y"], 1), (xn_st[0], 16), (xn_st[1], 16)):
                e.sem_inc(sem, n)

            e.wait_ge(s["cact_e"], 1)
            tsc(cact[:, 2, :], cact[:, 1, :], 1.0, ALU.add).then_inc(s["cact_1"], 1)
            e.wait_ge(s["cact_1"], 1)
            v.reciprocal(cact[:, 1, :], cact[:, 2, :]).then_inc(s["cact_1"], 1)
            e.wait_ge(s["cact_1"], 2)
            tt(cact[:, 3, :], cact[:, 0, :], cact[:, 1, :], ALU.mult).then_inc(s["cact_1"], 1)
            e.wait_ge(s["small_ld"], 16 * N_SMALL)
            for j in range(2):
                last = v.tensor_tensor_reduce(out=junk[1][:, j * DK:(j + 1) * DK], in0=lq[:, 2 * j, :], in1=lq[:, 2 * j + 1, :],
                                              scale=1.0, scalar=0.0, op0=ALU.mult, op1=ALU.add,
                                              accum_out=lam[:, j:j + 1])
            last.then_inc(s["lam_p"], 1)
            e.wait_ge(s["lam_e"], 1)
            tt(lam[:, 5:6], lam[:, 3:4], lam[:, 2:3], ALU.subtract).then_inc(s["lam_done"], 1)
            e.wait_ge(s["lam_done"], 1)
            tsc(lam[:, 4:5], lam[:, 5:6], -LAMBDA_INIT, ALU.add).then_inc(s["lam_done"], 1)

            n_rope = [0]

            def rope(ins):
                n_rope[0] += 1
                ins.then_inc(s["rope_step"], 1)
                e.wait_ge(s["rope_step"], n_rope[0])

            def wrapped(x, tmp):
                for op, lim, turn in ((ALU.is_gt, PI, -2 * np.pi), (ALU.is_lt, -PI, 2 * np.pi)):
                    rope(tsc(tmp, x, lim, op, float(turn), ALU.mult))
                    rope(tt(x, x, tmp, ALU.add))
                rope(tsc(x, x, PI, ALU.min, -PI, ALU.max))

            rope(v.tensor_copy(posf[:, :], pos[:, :]))
            angv = ang[:, 0, :].rearrange("p (t f) -> p t f", f=HALF)
            for f in range(HALF):
                last = tsc(angv[:, :, f], posf[:, :], INV_FREQ[f], ALU.mult)
            rope(last)
            rope(tsc(angi, ang[:, 0, :], float(1 / (2 * np.pi)), ALU.mult))
            rope(v.tensor_copy(ang[:, 1, :], angi))
            rope(stt(ang[:, 2, :], ang[:, 1, :], -TWO_PI_HI, ang[:, 0, :], ALU.mult, ALU.add))
            rope(stt(ang[:, 2, :], ang[:, 1, :], -TWO_PI_LO, ang[:, 2, :], ALU.mult, ALU.add))
            wrapped(ang[:, 2, :], ang[:, 1, :])
            rope(tsc(ang[:, 3, :], ang[:, 2, :], float(np.pi / 2), ALU.add))
            wrapped(ang[:, 3, :], ang[:, 1, :])
            e.sem_inc(s["rope_arg"], 1)

            e.wait_ge(s["rows_tr"], 1)
            v.tensor_copy(gcols[:, 0:19], bank(0)[:, 0:19])
            tsc(gcols[:, 19:20], bank(0)[:, 19:20], 1.0 - LAMBDA_INIT, ALU.mult).then_inc(s["rows_cols"], 1)

            def ada(g, j):
                n = g * KT + j
                e.wait_ge(ada_ld[j % 4], 16 * (2 * g + j // 4 + 1))
                e.wait_ge(s["ada_done"], n)
                stt(acc[:, g, :], aw[j % 4], cact[:, 3, j:j + 1], acc[:, g, :], ALU.mult, ALU.add).then_inc(s["ada_done"], 1)

            e.wait_ge(s["adab_ld"], 16)
            e.wait_ge(s["fills_done"], 2)
            e.wait_ge(s["cact_1"], 3)
            for j in range(KT):
                ada(0, j)
            e.wait_ge(s["mod1_ps"], 1)
            e.wait_ge(s["rows_cols"], 1)
            v.tensor_copy(S1[:, :], bank(1)[:, 0:KT])
            stt(A1[:, :], bank(1)[:, KT:2 * KT], 1.0, gcols[:, 0:KT], ALU.add, ALU.mult).then_inc(s["mod1_done"], 1)
            e.wait_ge(s["mod1_done"], 1)

            with e.Fori(0, NT // 2) as i:
                for u in range(2):
                    t = 2 * i + u
                    e.wait_ge(s["x_sd"], t + 1)
                    v.reciprocal(stat[:, 0, u:u + 1], stat[:, 1, u:u + 1]).then_inc(s["x_rs"], 1)
                    e.wait_ge(s["x_rs"], t + 1)
                    tsc(xb[u], xb[u], stat[:, 0, u:u + 1], ALU.mult).then_inc(s["x_norm"], 1)
                    e.wait_ge(s["x_tr"], t + 1)
                    for k in range(4):
                        last = tsc(hT[:, k, ds(t * P, P)], bank(4 + 2 * u)[:, k * P:(k + 1) * P],
                                   A1[:, k:k + 1], ALU.mult, S1[:, k:k + 1], ALU.add)
                    last.then_inc(s["h_evd"], 1)
            with e.Fori(1, 3) as g:
                for j in range(KT):
                    ada(g, j)

            with e.Fori(0, NT // 2) as i:
                for u in range(2):
                    t = 2 * i + u
                    e.wait_ge(s["qk_sq"], t + 1)
                    v.tensor_reduce(ssqk[:, ds(t * 16, 16)], junk[u].rearrange("p (c d) -> p c d", d=DK),
                                    AX.X, ALU.add).then_inc(s["qk_sum"], 1)
            e.wait_ge(s["qk_sd"], 1)
            v.reciprocal(rqk.rearrange("p t c -> p (t c)"), ssqk).then_inc(s["qk_rs"], 1)
            e.wait_ge(s["qk_rs"], 1)
            e.wait_ge(s["rope_sin"], 1)
            pre = ropeb[:, 0:256]
            x1, x2 = (pre.rearrange("p (c d) -> p c d", d=ROPE)[:, :, HALF * j:HALF * (j + 1)] for j in range(2))
            prod = [ropeb[:, 256 + 128 * j:384 + 128 * j].rearrange("p (c d) -> p c d", d=HALF) for j in range(4)]
            with e.Fori(0, NT) as t:
                qk = U[:, t, 0:1024].rearrange("p (c d) -> p c d", d=DK)
                tt(qk, qk, spread(rqk[:, t, :].rearrange("p (c o) -> p c o", o=1), [P, 16, DK]), ALU.mult).then_inc(s["qk_scaled"], 1)
                e.wait_ge(s["qk_scaled"], t + 1)
                tt(pre.rearrange("p (x h d) -> p x h d", x=2, h=8),
                   U[:, t, 0:1024].rearrange("p (x h d) -> p x h d", x=2, h=8)[:, :, :, 0:ROPE],
                   spread(gpre[:, :, :].rearrange("p x (o d) -> p x o d", o=1), [P, 2, 8, ROPE]), ALU.mult).then_inc(s["rope_in"], 1)
                e.wait_ge(s["rope_in"], t + 1)
                cos, sin = (spread(sincos[:, j, t, :].rearrange("p (o f) -> p o f", o=1), [P, 16, HALF]) for j in range(2))
                for o, a, b in zip(prod, (x1, x2, x2, x1), (cos, sin, cos, sin)):
                    last = tt(o, a, b, ALU.mult)
                last.then_inc(s["rope_prod"], 1)
                e.wait_ge(s["rope_prod"], t + 1)
                tt(qk[:, :, 0:HALF], prod[0], prod[1], ALU.subtract)
                tt(qk[:, :, HALF:ROPE], prod[2], prod[3], ALU.add).then_inc(s["rope_done"], 1)

            e.wait_ge(s["mods_ps"], 1)
            v.tensor_copy(S2[:, :], bank(0)[:, 0:KT])
            stt(A2[:, :], bank(0)[:, KT:2 * KT], 1.0, gcols[:, KT:2 * KT], ALU.add, ALU.mult).then_inc(s["mods_col"], 1)
            e.wait_ge(s["pad_st"], 80)
            for t in range(NT):
                e.wait_ge(s["qk_tr"], t + 1)
                tsc(kT[:, :, t * P:(t + 1) * P], bank(5 + 2 * (t % 2)).rearrange("p (h t) -> p h t", h=NH),
                    gcols[:, 17:18], ALU.mult).then_inc(s["kT_done"], 1)

            e.wait_ge(s["lam_done"], 2)
            score_v = PS[:, 0:4, :].rearrange("p (c b) n -> p c (b n)", c=2)
            with e.Fori(0, NH) as h:
                def row_max(i):
                    e.wait_ge(s["scores_ready"], h * NT + i + 2)
                    v.tensor_reduce(att_mx[:, i % 2, :], score_v[:, :, 0:(i + 1) * P], AX.X, ALU.max).then_inc(s["max_ready"], 1)
                    e.wait_ge(s["max_ready"], h * NT + i + 1)
                    tsc(att_nm[:, i % 2, :], att_mx[:, i % 2, :], -DK ** -0.5, ALU.mult).then_inc(s["nmax_ready"], 1)

                def combine(i):
                    n = (i + 1) * P
                    e.wait_ge(s["exp_done"], h * NT + i + 2)
                    e.wait_ge(s["att_o_done"], h * NT + i + 1)
                    v.reciprocal(att_rc[:, i % 2, 0:2], att_sum[:, i % 2, :]).then_inc(s["att_r"], 1)
                    e.wait_ge(s["att_r"], h * NT + i + 1)
                    stt(att_rc[:, i % 2, 2:3], att_rc[:, i % 2, 1:2], att_sum[:, i % 2, 0:1], lam[:, 4:5],
                        ALU.mult, ALU.mult).then_inc(s["att_nr"], 1)
                    e.wait_ge(s["att_nr"], h * NT + i + 1)
                    e.wait_ge(s["att_tr"], h * NT + i + 1)
                    stt(attn[i % 2][:, 0:n], E[:, i % 2, 1, 0:n], att_rc[:, i % 2, 2:3], E[:, i % 2, 0, 0:n],
                        ALU.mult, ALU.add).then_inc(s["att_a"], 1)

                def finish(i):
                    e.wait_ge(s["att_o"], h * NT + i + 3)
                    tsc(U[:, i, ds(h * DV, DV)], bank(6 + i % 2)[:, 0:DV], att_rc[:, i % 2, 0:1], ALU.mult).then_inc(s["att_o_done"], 1)

                row_max(0)
                for i in range(NT):
                    if i + 1 < NT:
                        row_max(i + 1)
                    combine(i)
                    if i >= 1:
                        finish(i - 1)
                finish(NT - 1)

            with e.Fori(0, NT // 2) as i:
                for u in range(2):
                    e.wait_ge(s["ob_sq"], 2 * i + u + 1)
                    v.tensor_reduce(sso[:, 0, ds((2 * i + u) * NH, NH)], junk[u][:, 0:HW].rearrange("p (c d) -> p c d", d=DV),
                                    AX.X, ALU.add).then_inc(s["ob_sum"], 1)
            e.wait_ge(s["ob_sd"], 1)
            v.reciprocal(sso[:, 0, :], sso[:, 0, :]).then_inc(s["ob_rs"], 1)
            e.wait_ge(s["ob_rs"], 1)
            with e.Fori(0, NT) as t:
                o = U[:, t, 0:HW].rearrange("p (c d) -> p c d", d=DV)
                tt(o, o, spread(sso[:, 0, ds(t * NH, NH)].rearrange("p (c o) -> p c o", o=1), [P, NH, DV]), ALU.mult).then_inc(s["ob_norm"], 1)

            e.wait_ge(s["z_step"], 3)
            stt(R2[:, 0:2048], bank(0, 4), 0.0, sp, ALU.min, ALU.subtract).then_inc(s["g_done"], 1)
            e.wait_ge(s["dec_done"], 1)
            e.wait_ge(s["gla_zero"], 1)
            e.wait_ge(s["proj_free"], 4 + 6 * NT)

            def gla_scale(t, u):
                e.wait_ge(s["gla_sc"], t + 1)
                stt(qin[u], U[:, t, 512:768], DK ** -0.5, EB[:, t, :], ALU.mult, ALU.mult)
                tt(kin[u], U[:, t, 768:1024], ENB[:, t, :], ALU.mult)
                tt(kdc[u], U[:, t, 768:1024], EKD[:, t, :], ALU.mult).then_inc(s["gla_in"], 1)

            def gla_state(t, u):
                v.tensor_copy(dcur[:, u, :], dec[:, ds(t * 4, 4)]).then_inc(s["gla_dec"], 1)
                e.wait_ge(s["gla_dec"], t + 1)
                e.wait_ge(s["gla_sc"], t + 3)
                e.wait_ge(s["gla_out_state"], t + 1)
                for pr in range(2):
                    last = stt(S_mid[u][:, pr, :], S_in[u][:, pr, :], dcur[:, u, 2 * pr:2 * pr + 1],
                               bank(3)[:, pr * DV:(pr + 1) * DV], ALU.mult, ALU.add)
                last.then_inc(s["gla_mid"], 1)
                e.wait_ge(s["gla_mid"], t + 1)
                e.wait_ge(s["gla_o"], t + 2)
                for pr in range(2):
                    last = stt(S_in[1 - u][:, pr, :], S_mid[u][:, pr, :], dcur[:, u, 2 * pr + 1:2 * pr + 2],
                               bank(4)[:, pr * DV:(pr + 1) * DV], ALU.mult, ALU.add)
                last.then_inc(s["gla_out_state"], 1)

            def gla_mask(t, u):
                wait_apart(e, (s["gla_att"], t + 1))
                for hd in range(NH):
                    last = v.copy_predicated(attS[u][:, hd, :], tri[:, :].bitcast(U32),
                                             bank(1 + hd % 2)[:, (hd // 2) * P:(hd // 2 + 1) * P])
                last.then_inc(s["gla_attS"], 1)

            gla_scale(0, 0)
            with e.Fori(0, NT // 2 - 1) as i:
                for u in range(2):
                    t = 2 * i + u
                    gla_scale(t + 1, 1 - u)
                    gla_state(t, u)
                    gla_mask(t, u)
            gla_scale(NT - 1, 1)
            for t in (NT - 2, NT - 1):
                gla_state(t, t % 2)
                gla_mask(t, t % 2)

            with e.Fori(0, NT // 2) as i:
                for u in range(2):
                    e.wait_ge(s["oa_sq"], 2 * i + u + 1)
                    v.tensor_reduce(sso[:, 1, ds((2 * i + u) * NH, NH)], junk[u][:, 0:HW].rearrange("p (c d) -> p c d", d=DV),
                                    AX.X, ALU.add).then_inc(s["oa_sum"], 1)
            e.wait_ge(s["oa_sd"], 1)
            v.reciprocal(sso[:, 1, :], sso[:, 1, :]).then_inc(s["oa_rs"], 1)
            e.wait_ge(s["oa_rs"], 1)
            e.wait_ge(s["oa_silu"], 1)
            with e.Fori(0, NT) as t:
                o = U[:, t, 1024:1536].rearrange("p (c d) -> p c d", d=DV)
                tt(o, o, spread(sso[:, 1, ds(t * NH, NH)].rearrange("p (c o) -> p c o", o=1), [P, NH, DV]), ALU.mult).then_inc(s["oa_n1"], 1)
                e.wait_ge(s["oa_n1"], t + 1)
                tt(U[:, t, 1024:1536], U[:, t, 1024:1536], U[:, t, 0:HW], ALU.mult).then_inc(s["oa_norm"], 1)

            e.wait_ge(s["oaT_done"], NT)
            with e.Fori(0, KT) as f:
                for half in range(2):
                    n = 2 * f + half
                    e.wait_ge(s["g_sig"], n + 1)
                    for x in range(2):
                        last = tt(sig[:, 2 * half + x, :], sig[:, 2 * half + x, :], bank(4 * half + 2 + x), ALU.mult)
                    last.then_inc(s["g_prod"], 1)
                    e.wait_ge(s["g_prod"], n + 1)
                    tt(mT[:, f, half * 512:(half + 1) * 512], sig[:, 2 * half, :], sig[:, 2 * half + 1, :], ALU.add).then_inc(s["g_free"], 1)

            with e.Fori(0, NT // 2) as i:
                for u in range(2):
                    t = 2 * i + u
                    e.wait_ge(s["mo_mm"], t + 3)
                    e.wait_ge(xn_st[u], 16 * (i + 1))
                    e.wait_ge(s["h2_tr"], t + 1)
                    tt(xn[u], bank(2 * u, 2), gate[:, 0, :], ALU.mult).then_inc(s["mo_gated"], 1)
                    e.wait_ge(s["mo_gated"], t + 3)
                    e.wait_ge(xh_ld[u], 16 * (i + 1))
                    tt(xh[u], xh[u], xn[u], ALU.add).then_inc(s["x1_ready"], 1)
                    e.wait_ge(s["x1_sd"], t + 1)
                    v.reciprocal(stat[:, 2, u:u + 1], stat[:, 3, u:u + 1]).then_inc(s["x1_rs"], 1)
                    e.wait_ge(s["h2_tr"], t + 3)
                    for k in range(4):
                        last = tsc(h2T[u][:, k, :], bank(4)[:, k * P:(k + 1) * P],
                                   A2[:, k:k + 1], ALU.mult, S2[:, k:k + 1], ALU.add)
                    last.then_inc(s["h2_evd"], 1)
                    e.wait_ge(s["rt_mm"], t + 3)
                    tt(logits[:, t, :], bank(6)[:, 0:NR], rbias[:, :], ALU.add).then_inc(s["rt_done"], 1)

            n_rt = [0]

            def rt(ins):
                n_rt[0] += 1
                ins.then_inc(s["rt_step"], 1)
                e.wait_ge(s["rt_step"], n_rt[0])

            def over(a, n):
                return spread(a.rearrange("p (t o) -> p t o", o=1), [P, NT, n])

            def first_max(x, n, m, eq, ids, oh):
                rt(v.tensor_reduce(m, x, AX.X, ALU.max))
                rt(tt(eq, x, over(m, n), ALU.is_equal))
                ids_b = spread(iota_e[:, 0:n].rearrange("p (o e) -> p o e", o=1), [P, NT, n])
                rt(stt(eq, eq, -float(NE), ids_b, ALU.mult, ALU.add))
                rt(v.tensor_reduce(ids, eq, AX.X, ALU.min))
                rt(tt(oh, eq, over(ids, n), ALU.is_equal))

            e.wait_ge(s["rt_done"], 1 + NT)
            lg = logits[:, :, 0:NG]
            le = logits[:, :, NG:NR]
            first_max(lg, NG, gm, eq_g, ids, oh_g)
            tt(rt_gd, lg, over(gm, NG), ALU.subtract).then_inc(s["rt_diff"], 1)
            e.wait_ge(s["rt_exp"], 1)
            rt(v.tensor_reduce(gsum, rt_gd, AX.X, ALU.add))
            rt(v.reciprocal(p_top, gsum))
            rt(tsc(oh_g, oh_g, -1.0, ALU.add, -NEG, ALU.mult))
            rt(tt(le.rearrange("p t (g x) -> p t g x", g=NG), le.rearrange("p t (g x) -> p t g x", g=NG),
                  spread(oh_g.rearrange("p t (g o) -> p t g o", o=1), [P, NT, NG, EPG]), ALU.add))
            first_max(le, NE, m1, eq_e, ids, oh1)
            rt(stt(le, oh1, 2 * NEG, le, ALU.mult, ALU.add))
            first_max(le, NE, m2, eq_e, ids, oh2)
            tt(rt_d[:, 0, :], m2, m1, ALU.subtract).then_inc(s["rt_diff"], 1)
            rt(tt(choice_b[:, 0:NT, :], oh1, oh2, ALU.add))
            rt(v.memset(choice_b[:, NT, :], 0.0))
            for t in range(NT):
                rt(tt(choice_b[:, NT + 1 + t, :], choice_b[:, NT + t, :], choice_b[:, t, :], ALU.add))
            e.sem_inc(s["rt_m"], 1)
            e.wait_ge(s["rt_exp"], 2)
            rt(tsc(gsum, rt_d[:, 1, :], 1.0, ALU.add))
            rt(v.reciprocal(gsum, gsum))
            wts = pack[:, :, :, :].bitcast(F32)
            rt(tt(gsum, gsum, p_top, ALU.mult))
            rt(v.tensor_copy(wts[:, 0, :, 1], gsum))
            rt(tt(wts[:, 1, :, 1], gsum, rt_d[:, 1, :], ALU.mult))
            e.wait_ge(s["rt_rank_mm"], 1)
            rt(v.tensor_copy(cnt, bank(1)[:, 0:NE]))
            big = R2[:, 4096:4096 + NE * NE]
            cmp = big[:, 0:NE * (NT - 1)].rearrange("p (x n) -> p x n", n=NT - 1)
            rt(tt(cmp, spread(cnt.rearrange("p (x o) -> p x o", o=1), [P, NE, NT - 1]),
                  spread(thr128[:, :].rearrange("p (o n) -> p o n", o=1), [P, NE, NT - 1]), ALU.is_gt))
            rt(v.tensor_reduce(extra, cmp, AX.X, ALU.add))
            sq = big.rearrange("p (x y) -> p x y", y=NE)
            e.wait_ge(s["mask0"], 6)
            rt(tt(sq, spread(extra.rearrange("p (o y) -> p o y", o=1), [P, NE, NE]), earlier, ALU.mult))
            rt(v.tensor_reduce(ovb, sq, AX.X, ALU.add))
            rt(stt(delta, ovb, float(NE - 1), pos_e[:, :], ALU.add, ALU.subtract))
            rt(tsc(delta, delta, float(P), ALU.mult))
            rank = bank(0)[:, 0:NT * NE].rearrange("p (t x) -> p t x", x=NE)
            rt(tsc(eq_e, rank, float(P), ALU.is_ge))
            rt(tt(eq_e, eq_e, spread(delta.rearrange("p (o x) -> p o x", o=1), [P, NT, NE]), ALU.mult))
            rt(tt(eq_e, eq_e, rank, ALU.add))
            rt(tsc(delta, pos_e[:, :], float(P), ALU.mult))
            rt(tt(eq_e, eq_e, spread(delta.rearrange("p (o x) -> p o x", o=1), [P, NT, NE]), ALU.add))
            for k, oh in enumerate((oh1, oh2)):
                rt(tt(oh, oh, eq_e, ALU.mult))
                rt(v.tensor_reduce(ids, oh, AX.X, ALU.add))
                rt(v.tensor_copy(dest_i[:, k * NT:(k + 1) * NT], ids))
            e.sem_inc(s["rt_dest"], 1)
            rt(tt(ovb, ovb, extra, ALU.add))
            ends = big[:, 0:MAXOV * NE].rearrange("p (j x) -> p j x", x=NE)
            rt(tt(ends, spread(ovb.rearrange("p (o x) -> p o x", o=1), [P, MAXOV, NE]),
                  spread(thr[:, :].rearrange("p (j o) -> p j o", o=1), [P, MAXOV, NE]), ALU.is_le))
            rt(v.tensor_reduce(ovf_f[:, 0:MAXOV], ends, AX.X, ALU.add))
            rt(tsc(ovf_f[:, 0:MAXOV], ovf_f[:, 0:MAXOV], float(NE - 1), ALU.min))
            rt(v.tensor_copy(ovf_f[:, MAXOV:MAXOV + 1], ovb[:, NE - 1:NE]))
            v.tensor_copy(ovf[:, :], ovf_f).then_inc(s["ovf_ready"], 1)

            def rows_read(n, u):
                e.wait_ge(s["m_tr"], n + 3)
                for k in range(4):
                    last = tsc(xT[u][:, k, :], bank(0)[:, k * P:(k + 1) * P],
                               A2[:, k:k + 1], ALU.mult, S2[:, k:k + 1], ALU.add)
                last.then_inc(s["m_evd"], 1)

            def hidden(n):
                e.wait_ge(s["m_silu"], n + 1)
                e.wait_ge(s["m2_tr"], n + 1)
                tt(hh, sg, bank(3), ALU.mult).then_inc(s["m_hh"], 1)

            def weighted(n, u):
                v.tensor_copy(wt[:, u:u + 1], tab[:, ds(n, 1), 1:2].rearrange("p b c -> p (b c)").bitcast(F32)).then_inc(s["m_wt"], 1)
                e.wait_ge(s["m_wt"], n + 1)
                e.wait_ge(s["m2_mm"], n + 2)
                e.wait_ge(s["tis_ready"], n + 1)
                stt(yb[u], bank(6, 2), wt[:, u:u + 1], gate[:, 1, :], ALU.mult, ALU.mult).then_inc(s["m_y"], 1)

            rows_read(0, 0)
            hidden(0)
            rows_read(1, 1)
            with e.Fori(0, NE // 2 - 1) as i:
                for u in (1, 0):
                    n = 2 * i + 2 - u
                    hidden(n)
                    rows_read(n + 1, 1 - u)
                    weighted(n - 1, 1 - u)
            hidden(NE - 1)
            weighted(NE - 2, 0)
            weighted(NE - 1, 1)
            e.wait_ge(s["ovf_ready"], 1)
            n_ov = e.value_load(ovf[0:1, MAXOV:MAXOV + 1], min_val=0, max_val=MAXOV)
            with e.If(n_ov > 0):
                with e.Fori(0, n_ov) as j:
                    rows_read(NE + j, 0)
                    hidden(NE + j)
                    weighted(NE + j, 0)


_INS = ["x", "c", "positions", "ada_w", "ada_b", "norm1_g", "norm2_g", "w_in", "gla_alpha_up", "gla_alpha_b",
        "gla_out_g", "diff_q_g", "diff_k_g", "diff_lq1", "diff_lk1", "diff_lq2", "diff_lk2", "diff_out_g",
        "w_branch_a", "w_branch_b", "w_out", "router_group_w", "router_group_b", "router_expert_w",
        "router_expert_b", "expert_w1", "expert_w3", "expert_w2"]


def kernel(**inputs):
    import concourse.bacc as bacc
    from concourse.bass_utils import run_bass_kernel_spmd

    nc = bacc.Bacc("TRN2", target_bir_lowering=False, num_devices=1)
    arrays, io = {}, {}
    for name in _INS:
        a = np.ascontiguousarray(inputs[name])[0]
        arrays[f"in_{name}"] = a
        io[name] = nc.dram_tensor(f"in_{name}", a.shape, mybir.dt.from_np(a.dtype), kind="ExternalInput").ap()
    out = nc.dram_tensor("out_rows", (T + PAD, D), F32, kind="ExternalOutput").ap()
    build(nc, io, out)
    r = run_bass_kernel_spmd(nc, [arrays], core_ids=[0])
    return r.results[0]["out_rows"][:T].reshape(1, T, D)
```

```python
from contextlib import ExitStack

import numpy as np
import concourse.bass as bass
from concourse import mybir

ALU = mybir.AluOpType
ACT = mybir.ActivationFunctionType
AX = mybir.AxisListType
F32 = mybir.dt.float32
BF16 = mybir.dt.bfloat16
I32 = mybir.dt.int32
U32 = mybir.dt.uint32
ds = bass.ds

P = 128
T = 1024
D = 1024
NT = T // P
KT = D // P
NH = 4
DK = 64
DV = 128
HW = NH * DV
RANK = 16
CH = 64
TAU = 16.0
ROPE = 16
HALF = ROPE // 2
THETA = 500000.0
EPS = 1e-6
LAMBDA_INIT = 0.8 - 0.6 * float(np.exp(-0.3 * 0))
NEG = -1e30
NG, EPG = 4, 8
NE = NG * EPG
NR = NG + NE
MAXOV = (2 * T) // P - 1
NBLK = NE + MAXOV
PAD = 2 * P
O_GQK, O_GV, O_GR, O_GLR = 0, 512, 1024, 1536
O_DQ, O_DK, O_DV, O_GA, O_GB = 1552, 2064, 2576, 3088, 4112
INV_FREQ = [float(f) for f in
            (np.float32(THETA) ** (-np.arange(HALF, dtype=np.float32) / np.float32(HALF)))]
TWO_PI_HI = 6.28125
TWO_PI_LO = float(2 * np.pi - 6.28125)
PI = 3.14159

SEMS = """
c_ld early_ld small_ld fills_done consts_done mask0 ada_ld0 ada_ld1 ada_ld2 ada_ld3 ada_done
cact_e cact_1 rows_tr rows_cols mod1_ps mod1_done rope_step rope_arg rope_sin
lam_p lam_e lam_done
x_ld0 x_ld1 x_sq x_sd x_rs x_norm x_tr h_evd h_eva
w_ld proj_mm proj_free
qk_sq qk_sum qk_sd qk_rs qk_scaled rope_in rope_prod rope_done
mods_ps mods_col gates_done qk_tr qT_done kT_done
head_staged scores_ready max_ready nmax_ready exp_done att_r att_nr att_a att_tr aT_done att_o att_o_done
out_sd out_rs ob_sq ob_norm ob_tr obT_done
alr_ones glr_mm glr_done gv_moved z_mm z_step g_done cum_mm dec_mm eb_done dec_done
gla_zero gla_dec gla_in gla_vcopy gla_tr gla_qkT gla_att gla_attS gla_sc gla_mid gla_out_state gla_o gla_o_done
oa_sq oa_sum oa_n1 oa_silu oa_norm oa_tr oaT_done
gw_ld0 gw_ld1 early_mm early_sig g_mm g_sig g_prod g_free
wout_ld xh_ld0 xh_ld1 ms_ready mo_mm mo_gated x1_ready x1_sq x1_sd x1_rs xn2_ready x1_st0 x1_st1 xn_st0 xn_st1 h2_tr h2_evd h2_eva rt_mm rt_done
rt_step rt_diff rt_exp rt_m rt_sums_mm slots_in
pad_st tab_done
w13_ld0 w13_ld1 w2_ld0 w2_ld1 tig_ready tis_ready xg_ld0 xg_ld1 m_tr m_evd m_eva m1_mm m_silu m_hh m2_tr m_hhT m2_mm m_wt m_y sc_done0 sc_done1
ovf_ready
""".split()


N_EARLY = 9
N_SMALL = 14


def build(nc, io, out):
    with ExitStack() as ctx:
        def sb(name, shape, dt=F32):
            return ctx.enter_context(nc.sbuf_tensor(name, shape, dt))

        s = {n: ctx.enter_context(nc.semaphore(n)) for n in SEMS}
        ada_ld = [s["ada_ld0"], s["ada_ld1"], s["ada_ld2"], s["ada_ld3"]]
        x_ld, xh_ld = [s["x_ld0"], s["x_ld1"]], [s["xh_ld0"], s["xh_ld1"]]
        gw_ld, w13_ld, w2_ld, xg_ld = ([s["gw_ld0"], s["gw_ld1"]], [s["w13_ld0"], s["w13_ld1"]],
                                       [s["w2_ld0"], s["w2_ld1"]], [s["xg_ld0"], s["xg_ld1"]])
        sc_done = [s["sc_done0"], s["sc_done1"]]
        x1_st, xn_st = [s["x1_st0"], s["x1_st1"]], [s["xn_st0"], s["xn_st1"]]

        xn_rows = nc.dram_tensor("xn_rows", [T + PAD, D], F32, kind="Internal").ap()

        PS = ctx.enter_context(nc.psum_tensor("PS", [P, 8, 512], F32))

        def bank(b, n=1):
            return PS[:, b:b + n, :].rearrange("p b n -> p (b n)")

        R1 = sb("R1", [P, 12288])
        HT = sb("HT", [P, 8192])
        R2 = sb("R2", [P, 8192])
        R3 = sb("R3", [P, 8192])
        R4 = sb("R4", [P, 8192])
        WK = sb("WK", [P, 4096])

        ident = sb("ident", [P, P])
        identb = sb("identb", [P, P], BF16)
        causal_neg = sb("causal_neg", [P, P], BF16)
        tri = sb("tri", [P, P])
        blk = sb("blk", [P, P])
        suf = sb("suf", [P, P])
        onesf = sb("onesf", [P, P])
        iota_e = sb("iota_e", [P, NE])
        pos_e = sb("pos_e", [P, NE])
        thr = sb("thr", [P, MAXOV])
        thr128 = sb("thr128", [P, NT - 1])
        gcols = sb("gcols", [P, 20])
        gpre = sb("gpre", [P, 2, ROPE])
        lam = sb("lam", [P, 8])
        rbias = sb("rbias", [P, NR])
        wr = sb("wr", [P, KT, NR])
        pos = sb("pos", [P, NT], I32)
        posf = sb("posf", [P, NT])
        cact = sb("cact", [P, 4, KT])
        S1 = sb("S1", [P, KT])
        A1 = sb("A1", [P, KT])
        S2 = sb("S2", [P, KT])
        A2 = sb("A2", [P, KT])
        gate = sb("gate", [P, 2, D])
        stat = sb("stat", [P, 4, 2])
        att_mx = sb("att_mx", [P, 2, 2])
        att_nm = sb("att_nm", [P, 2, 2])
        att_sum = sb("att_sum", [P, 2, 2])
        att_rc = sb("att_rc", [P, 2, 3])
        sso = sb("sso", [P, 2, NT * NH])
        xstat = sso[:, 1, 0:2 * NT].rearrange("p (x t) -> p x t", x=2)
        dec = sb("dec", [P, NT * 4])
        dcur = sb("dcur", [P, 2, 4])
        wts = sb("wts", [P, 2 * NT])
        tig = sb("tig", [P, 2, 1], I32)
        tis = sb("tis", [P, 2, 1], I32)
        wt = sb("wt", [P, 2])
        ovf = sb("ovf", [P, MAXOV + 1], I32)

        def rt_tile(name, *shape):
            return sb(name, [P, *shape])

        gm, ids, gsum, p_top, m1, m2 = (rt_tile(n, NT)[:, :] for n in ("rt_gm", "rt_ids", "rt_gsum", "rt_ptop", "rt_m1", "rt_m2"))
        cnt, extra, ovb, delta, ovf_f = (R2[:, 3584 + 32 * j:3616 + 32 * j] for j in range(5))
        ovf_f = ovf_f[:, 0:MAXOV + 1]
        rt_d = rt_tile("rt_dm", 2, NT)
        wide = R2[:, 0:2048].rearrange("p (x t n) -> p x t n", x=8, t=NT)
        eq_e, oh1, oh2 = (wide[:, j] for j in range(3))
        eq_g, oh_g, rt_gd = (wide[:, 3 + j, :, 0:NG] for j in range(3))

        small_w = sb("small_w", [P, 384])
        aup = small_w[0:RANK + 1, 0:256]
        wlr = small_w[:, 256:384].rearrange("p (k n) -> p k n", k=KT)
        logits = small_w[:, 0:NT * NR].rearrange("p (t n) -> p t n", t=NT)
        NB1 = NBLK + 1
        d1 = WK[:, 2048:4096].rearrange("p (c s) -> p c s", c=2 * NT)
        d2 = R2[:, 5120:5120 + 2 * NT * 3 * NBLK].rearrange("p (c x b) -> p c x b", c=2 * NT, x=3)
        past = R4[:, 7296:7296 + 2 * NT * NB1].rearrange("p (c b) -> p c b", c=2 * NT)
        slot_row = R2[:, 7424:7552]
        pad_tok = R2[:, 7552:7552 + NBLK]
        starts = R2[:, 7600:7600 + NB1]
        tok_col = R2[:, 7856:7856 + 2 * NT]
        slot_row_i, pad_tok_i, starts_i, tok_i = (R4[:, 8064:8192].bitcast(I32), R2[:, 7648:7648 + NB1].bitcast(I32),
                                                  R2[:, 7696:7696 + NB1].bitcast(I32), R2[:, 7840:7856].bitcast(I32))
        dest, past_n = R2[:, 7872:7888], R2[:, 7888:7904]
        tab_tok = R2[:, 7744:7744 + NBLK].bitcast(I32)
        tab_w = R2[:, 7792:7792 + NBLK]
        tab_gap = R2[:, 7904:7904 + NBLK]
        ang = R2[:, 6272:6528].rearrange("p (x n) -> p x n", x=4)
        iota_i = R2[:, 6592:6624].bitcast(I32)
        pos_i = R2[:, 6624:6656].bitcast(I32)
        onesb = R4[:, 7168:7232].bitcast(BF16)
        before = R4[:, 7232:7296].bitcast(BF16)
        angi = R2[:, 6528:6592].bitcast(I32)
        lq = R2[:, 6656:6912].rearrange("p (x n) -> p x n", x=4)
        rows = R2[0:20, 6912:7040]
        sincos = R2[:, 7040:7168].rearrange("p (x t f) -> p x t f", x=2, t=NT)
        ssqk = WK[:, 768:896]
        rqk = WK[:, 896:1024].rearrange("p (t c) -> p t c", t=NT)
        choice_b = R2[:, 3072:3072 + (2 * NT + 1) * NE // 2].bitcast(BF16).rearrange("p (t n) -> p t n", n=NE)
        U = R1[:, :].rearrange("p (t n) -> p t n", t=NT)
        hT = HT[:, :].rearrange("p (k t) -> p k t", k=KT)
        acc = R2[:, 0:6144].rearrange("p (g n) -> p g n", g=3)
        aw = [R4[:, 2048 * i:2048 * (i + 1)] for i in range(4)]
        wring = R3[:, :].rearrange("p (r k n) -> p r k n", r=2, k=KT)
        x_all = R1[:, 0:8192].rearrange("p (t n) -> p t n", t=NT)
        ropeb = WK[:, 0:768]
        junk = [WK[:, 2048 + 1024 * i:2048 + 1024 * (i + 1)] for i in range(2)]
        qT = R2[:, 0:4096].rearrange("p (h t) -> p h t", h=NH)
        kT = R2[:, 4096:8192].rearrange("p (h t) -> p h t", h=NH)
        qs, ks = R4[:, 0:1024], R4[:, 1024:2048]
        E = R4[:, 2048:6144].rearrange("p (u c n) -> p u c n", u=2, c=2)
        attn = [R4[:, 6144 + 1024 * i:6144 + 1024 * (i + 1)] for i in range(2)]
        attnT = [WK[:, 1024 * i:1024 * (i + 1)] for i in range(2)]
        oaT = R4[:, 0:4096].rearrange("p (h t) -> p h t", h=NH)
        obT = R4[:, 4096:8192].rearrange("p (h t) -> p h t", h=NH)
        alrT = WK[0:RANK + 1, 2048:3072]
        gv_tmp = R2[:, 4096:8192].rearrange("p (t n) -> p t n", t=NT)
        o_att = R2[:, 0:4096].rearrange("p (h t d) -> p h t d", h=NH, t=NT)
        sp = R4[:, 1024:3072]
        EB, ENB, EKD = (R2[:, 2048 * i:2048 * (i + 1)].rearrange("p (t n) -> p t n", t=NT)
                        for i in range(1, 4))
        gl = [WK[:, 0:2304], R4[:, 0:2304]]
        qin, kin, kdc, vcp = ([g[:, 0:256] for g in gl], [g[:, 256:512] for g in gl],
                              [g[:, 512:768] for g in gl], [g[:, 768:1280] for g in gl])
        qkT = [g[:, 1280:1792].rearrange("p (x t) -> p x t", x=4) for g in gl]
        attS = [g[:, 1792:2304].rearrange("p (h t) -> p h t", h=4) for g in gl]
        S_in = [R4[:, 2304 + 256 * i:2560 + 256 * i].rearrange("p (h v) -> p h v", h=2) for i in range(2)]
        S_mid = [R4[:, 2816 + 256 * i:3072 + 256 * i].rearrange("p (h v) -> p h v", h=2) for i in range(2)]
        gw = [R3[:, 3072 * i:3072 * (i + 1)].rearrange("p (k n) -> p k n", k=24) for i in range(2)]
        sig = R3[:, 6144:8192].rearrange("p (x n) -> p x n", x=4)
        early = [[[WK[:, 2304 + 512 * half:2816 + 512 * half] for half in range(2)],
                  [R2[:, 512 * half:512 * (half + 1)] for half in range(2)]],
                 [[sig[:, 2 * half + x, :] for half in range(2)] for x in range(2)]]
        mT = R2[:, :].rearrange("p (k t) -> p k t", k=KT)
        wout = R1[:, 0:8192].rearrange("p (k n) -> p k n", k=KT)
        xh = [R4[:, 4096 + 1024 * i:5120 + 1024 * i] for i in range(2)]
        ms = [R4[:, 6144 + 1024 * i:7168 + 1024 * i].rearrange("p (k t) -> p k t", k=KT) for i in range(2)]
        xn = [WK[:, 1024 * i:1024 * (i + 1)] for i in range(2)]
        h2T = [WK[:, 2048 + 1024 * i:3072 + 1024 * i].rearrange("p (k t) -> p k t", k=KT) for i in range(2)]
        earlier = R4[:, 6144:7168].rearrange("p (x y) -> p x y", y=NE)
        w13 = [HT[:, :].rearrange("p (w k n) -> p w k n", w=2, k=KT),
               R3[:, :].rearrange("p (w k n) -> p w k n", w=2, k=KT)]
        w2b = [R1[:, 8192:12288].rearrange("p (k n) -> p k n", k=4),
               R4[:, 0:4096].rearrange("p (k n) -> p k n", k=4)]
        xg = [R2[:, 1024 * i:1024 * (i + 1)] for i in range(2)]
        xT = [R2[:, 2048 + 1024 * i:3072 + 1024 * i].rearrange("p (k t) -> p k t", k=KT) for i in range(2)]
        yb = [R2[:, 4096 + 1024 * i:5120 + 1024 * i] for i in range(2)]
        sg, hh = R2[:, 6144:6656], R2[:, 6656:7168]
        hhT = R2[:, 7168:7680].rearrange("p (k t) -> p k t", k=4)
        zrow = R2[:, 7168:8192]

        w_in_v = io["w_in"].rearrange("(k p) n -> p k n", p=P)
        ada_v = io["ada_w"].rearrange("(p j) n -> p j n", j=KT)
        x_v = io["x"].rearrange("(t p) n -> t p n", p=P)
        out_v = out.rearrange("(t p) n -> t p n", p=P)
        xn_v = xn_rows.rearrange("(t p) n -> t p n", p=P)
        w1_v = io["expert_w1"].rearrange("e (k p) n -> e p k n", p=P)
        w3_v = io["expert_w3"].rearrange("e (k p) n -> e p k n", p=P)
        w2_v = io["expert_w2"].rearrange("e (k p) n -> e p k n", p=P)

        def vec(name):
            return io[name].rearrange("(a n) -> a n", a=1)

        def wait_apart(e, *waits):
            values = [v if isinstance(v, int) else e.to_reg(v) for _, v in waits]
            e.wait_ge(s["consts_done"], 1)
            for (sem, _), v in zip(waits, values):
                e.wait_ge(sem, v)

        def expert_of(n):
            return (n % NG) * EPG + n // NG

        block = ctx.enter_context(nc.Block())

        @block.sync
        def _(sp_):
            e = sp_
            n_small = {"early_ld": 0, "small_ld": 0}

            def small(dst, src, loaded="small_ld"):
                n_small[loaded] += 1
                e.dma_start(dst, src, allow_slow_non_contiguous=True).then_inc(s[loaded], 16)

            def load_ada(g, j, dynamic):
                if dynamic or g * KT + j >= 4:
                    e.wait_ge(s["ada_done"], g * KT + j - 3)
                e.dma_start(aw[j % 4], ada_v[:, j, ds(g * 2048, 2048)]).then_inc(ada_ld[j % 4], 16)

            e.dma_start(cact[:, 0, :], io["c"].rearrange("(p j) -> p j", j=KT)).then_inc(s["c_ld"], 16)
            load_ada(0, 0, False)
            load_ada(0, 1, False)
            e.wait_ge(s["fills_done"], 1)
            small(rows[0:8, :], io["norm1_g"].rearrange("(k p) -> k p", p=P), "early_ld")
            small(rows[8:16, :], io["norm2_g"].rearrange("(k p) -> k p", p=P), "early_ld")
            for r, nm in ((16, "diff_q_g"), (17, "diff_k_g")):
                for c in range(2):
                    small(rows[r:r + 1, c * DK + ROPE:(c + 1) * DK], vec(nm)[:, ROPE:DK], "early_ld")
            small(rows[18:19, :], vec("gla_out_g"), "early_ld")
            small(rows[19:20, :], vec("diff_out_g"), "early_ld")
            e.wait_ge(s["fills_done"], 2)
            small(acc[0:1, :, :], vec("ada_b").rearrange("a (g n) -> a g n", g=3), "early_ld")

            def load_x(g):
                e.dma_start(x_all[:, 4 * g:4 * g + 4, :],
                            x_v[4 * g:4 * g + 4].rearrange("t p n -> p t n")).then_inc(x_ld[g], 16)

            for j in range(2, KT - 2):
                load_ada(0, j, False)
            load_x(0)
            for j in range(KT - 2, KT):
                load_ada(0, j, False)
            load_x(1)
            e.dma_start(wring[:, 0], w_in_v[:, :, O_DQ:O_DQ + HW]).then_inc(s["w_ld"], 16)
            small(pos[:, :], io["positions"].rearrange("(t p) -> p t", p=P))
            small(gpre[:, 0, :], io["diff_q_g"][0:ROPE].partition_broadcast(P))
            small(gpre[:, 1, :], io["diff_k_g"][0:ROPE].partition_broadcast(P))
            for j, nm in enumerate(("diff_lq1", "diff_lk1", "diff_lq2", "diff_lk2")):
                small(lq[:, j, :], io[nm].partition_broadcast(P))
            small(rbias[:, 0:NG], io["router_group_b"].partition_broadcast(P))
            small(rbias[:, NG:NR], io["router_expert_b"].partition_broadcast(P))
            small(wr[:, :, 0:NG], io["router_group_w"].rearrange("(k p) n -> p k n", p=P))
            small(wr[:, :, NG:NR], io["router_expert_w"].rearrange("(k p) n -> p k n", p=P))
            small(aup[0:RANK, :], io["gla_alpha_up"])
            small(aup[RANK:RANK + 1, :], vec("gla_alpha_b"))
            small(wlr, w_in_v[:, :, O_GLR:O_GLR + RANK])
            assert n_small == {"early_ld": N_EARLY, "small_ld": N_SMALL}
            e.wait_ge(s["w_ld"], 16)
            e.dma_start(wring[:, 1], w_in_v[:, :, O_DK:O_DK + HW]).then_inc(s["w_ld"], 16)
            with e.Fori(1, 3) as g:
                for j in range(KT):
                    load_ada(g, j, True)
            e.wait_ge(s["consts_done"], 1)
            for u in range(2):
                e.dma_start(out_v[NT + u], zrow).then_inc(s["pad_st"], 16)
                e.dma_start(xn_v[NT + u], zrow).then_inc(s["pad_st"], 16)
            for n, off in ((2, O_DV), (3, O_GQK), (4, O_GR), (5, O_GV)):
                e.wait_ge(s["w_ld"], 16 * n)
                e.wait_ge(s["proj_mm"], NT * (n - 1))
                e.dma_start(wring[:, n % 2], w_in_v[:, :, off:off + HW]).then_inc(s["w_ld"], 16)
            def load_gw(u, f):
                for k0, nk, src in ((0, 8, w_in_v[:, :, ds(O_GA + f * P, P)]),
                                    (8, 8, w_in_v[:, :, ds(O_GB + f * P, P)]),
                                    (16, 4, io["w_branch_a"].rearrange("(k p) n -> p k n", p=P)[:, :, ds(f * P, P)]),
                                    (20, 4, io["w_branch_b"].rearrange("(k p) n -> p k n", p=P)[:, :, ds(f * P, P)])):
                    e.dma_start(gw[u][:, k0:k0 + nk, :], src).then_inc(gw_ld[u], 16)

            e.wait_ge(s["w_ld"], 16 * 6)
            e.wait_ge(s["proj_mm"], NT * 5)
            load_gw(0, 1)
            e.wait_ge(s["proj_mm"], NT * 6)
            load_gw(1, 0)
            for u in range(2):
                e.wait_ge(s["g_mm"], 2 * u + 2)
                load_gw(u, u + 2)
            with e.Fori(2, KT // 2) as i:
                for u in range(2):
                    e.wait_ge(s["g_free"], 2 * (2 * i + u) + 2)
                    load_gw(u, 2 * i + u)
            e.wait_ge(s["oa_norm"], NT)
            e.wait_ge(s["oa_tr"], NT)
            e.dma_start(wout, io["w_out"].rearrange("(k p) n -> p k n", p=P)).then_inc(s["wout_ld"], 16)
            e.dma_start(w2b[0], w2_v[0]).then_inc(w2_ld[0], 16)
            e.wait_ge(s["g_mm"], 2 * KT)
            e.wait_ge(s["g_free"], 4 + 2 * KT)
            for u in range(2):
                e.dma_start(xh[u], x_v[u]).then_inc(xh_ld[u], 16)
            e.dma_start(w13[0][:, 0], w1_v[0]).then_inc(w13_ld[0], 16)
            e.dma_start(w13[0][:, 1], w3_v[0]).then_inc(w13_ld[0], 16)
            e.dma_start(w13[1][:, 0], w1_v[expert_of(1)]).then_inc(w13_ld[1], 16)
            e.dma_start(w13[1][:, 1], w3_v[expert_of(1)]).then_inc(w13_ld[1], 16)
            e.dma_start(w2b[1], w2_v[expert_of(1)]).then_inc(w2_ld[1], 16)

            def store_x(t, u):
                e.wait_ge(s["x1_ready"], t + 1)
                e.dma_start(out_v[t], xh[u]).then_inc(x1_st[u], 16)
                e.wait_ge(s["xn2_ready"], t + 1)
                e.dma_start(xn_v[t], xn[u]).then_inc(xn_st[u], 16)

            with e.Fori(0, NT // 2 - 1) as i:
                for u in range(2):
                    store_x(2 * i + u, u)
                    e.wait_ge(x1_st[u], 16 * (i + 1))
                    e.wait_ge(s["x1_sq"], 2 * i + u + 1)
                    e.dma_start(xh[u], x_v[2 * i + u + 2]).then_inc(xh_ld[u], 16)
            for u in range(2):
                store_x(NT - 2 + u, u)
            def load_w13(u, n, ex):
                e.wait_ge(s["m1_mm"], n - 1)
                e.dma_start(w13[u][:, 0], w1_v[ex]).then_inc(w13_ld[u], 16)
                e.dma_start(w13[u][:, 1], w3_v[ex]).then_inc(w13_ld[u], 16)

            def load_w2(u, n, ex):
                e.wait_ge(s["m2_mm"], n)
                e.dma_start(w2b[u], w2_v[ex]).then_inc(w2_ld[u], 16)

            for n in (2, 3):
                load_w13(n % 2, n, expert_of(n))
                load_w2(n % 2, n, expert_of(n))
            with e.Fori(1, EPG) as i:
                for g in range(NG):
                    load_w13(g % 2, NG * i + g, EPG * g + i)
                    load_w2(g % 2, NG * i + g, EPG * g + i)
            e.wait_ge(s["ovf_ready"], 1)
            n_ov = e.value_load(ovf[0:1, MAXOV:MAXOV + 1], min_val=0, max_val=MAXOV)
            with e.If(n_ov > 0):
                with e.Fori(0, n_ov) as j:
                    ex = e.value_load(ovf[0:1, ds(j, 1)], min_val=0, max_val=NE - 1)
                    e.wait_ge(s["m2_mm"], NE + j + 1)
                    e.dma_start(w13[0][:, 0], w1_v[ex]).then_inc(w13_ld[0], 16)
                    e.dma_start(w13[0][:, 1], w3_v[ex]).then_inc(w13_ld[0], 16)
                    e.dma_start(w2b[0], w2_v[ex]).then_inc(w2_ld[0], 16)
            for u in range(2):
                e.wait_ge(x1_st[u], 16 * NT // 2)
                e.wait_ge(xn_st[u], 16 + 16 * NT // 2)
            e.wait_ge(s["pad_st"], 64)

        @block.gpsimd
        def _(e):
            e.memset(rows, 1.0)
            e.memset(aup, 0.0).then_inc(s["fills_done"], 1)
            e.memset(R2[:, 0:6144], 0.0).then_inc(s["fills_done"], 1)
            e.memset(zrow, 0.0)
            e.memset(ident[:, :], 0.0)
            e.memset(causal_neg[:, :], 0.0)
            e.memset(tri[:, :], 1.0 / TAU)
            e.memset(blk[:, :], 0.0)
            e.memset(onesf[:, :], 1.0)
            e.iota(pos_i, pattern=[[1, NG], [NG, EPG]], base=0, channel_multiplier=0)
            e.iota(iota_i, pattern=[[1, NE]], base=0, channel_multiplier=0).then_inc(s["mask0"], 1)
            e.wait_ge(s["mask0"], 1)
            e.affine_select(out=ident[:, :], in_=ident[:, :], compare_op=ALU.not_equal, fill=1.0,
                            base=0, pattern=[[-1, P]], channel_multiplier=1)
            e.affine_select(out=causal_neg[:, :], in_=causal_neg[:, :], compare_op=ALU.is_ge, fill=NEG,
                            base=0, pattern=[[-1, P]], channel_multiplier=1)
            e.affine_select(out=tri[:, :], in_=tri[:, :], compare_op=ALU.is_ge, fill=0.0,
                            base=0, pattern=[[1, P]], channel_multiplier=-1)
            for n in range(NT - 1):
                e.memset(thr128[:, n:n + 1], float(P * (n + 1)))
            e.tensor_copy(iota_e[:, :], iota_i)
            e.tensor_copy(pos_e[:, :], pos_i)
            e.tensor_copy(thr[:, :], iota_i[:, 0:MAXOV]).then_inc(s["mask0"], 1)
            e.wait_ge(s["mask0"], 2)
            e.memset(tri[0:CH, CH:P], 0.0)
            e.memset(blk[0:CH, 0:CH], 1.0 / TAU)
            e.tensor_copy(identb[:, :], ident[:, :]).then_inc(s["mask0"], 1)
            e.wait_ge(s["mask0"], 3)
            e.memset(blk[CH:P, CH:P], 1.0 / TAU).then_inc(s["mask0"], 1)
            e.wait_ge(s["mask0"], 4)
            e.tensor_sub(suf[:, :], blk[:, :], tri[:, :]).then_inc(s["consts_done"], 1)

            e.wait_ge(s["qT_done"], NT)
            e.wait_ge(s["kT_done"], NT)

            def stage_head(h):
                wait_apart(e, (s["scores_ready"], h * NT + 1))
                e.tensor_copy(qs, qT[:, h, :])
                e.tensor_copy(ks, kT[:, h, :]).then_inc(s["head_staged"], 1)

            e.memset(WK[0:32, 2048:3072], 1.0).then_inc(s["alr_ones"], 1)
            with e.Fori(1, NH) as h:
                stage_head(h)

            e.wait_ge(s["dec_mm"], 1)
            e.wait_ge(s["obT_done"], NT)
            e.memset(attS[0], 0.0)
            e.memset(attS[1], 0.0)
            e.memset(S_in[0], 0.0).then_inc(s["gla_zero"], 1)
            e.wait_ge(s["gv_moved"], 1)
            with e.Fori(0, NT // 2) as i:
                for u in range(2):
                    t = 2 * i + u
                    wait_apart(e, (s["gla_o"], t + 1))
                    e.tensor_copy(vcp[u], U[:, t, 1024:1536]).then_inc(s["gla_vcopy"], 1)

            def stage_merged(t, u):
                wait_apart(e, (s["mo_mm"], t + 1))
                e.tensor_copy(ms[u], mT[:, :, ds(t * P, P)]).then_inc(s["ms_ready"], 1)

            e.wait_ge(s["g_free"], 4 + 2 * KT)
            stage_merged(1, 1)
            with e.Fori(1, NT // 2) as i:
                for u in range(2):
                    stage_merged(2 * i + u, u)

            e.wait_ge(s["mo_mm"], 2 + NT)
            e.memset(onesb, 1.0)
            e.memset(before, 1.0)
            e.memset(earlier, 1.0).then_inc(s["mask0"], 1)
            e.wait_ge(s["mask0"], 5)
            e.affine_select(out=before, in_=before, compare_op=ALU.is_gt, fill=0.0,
                            base=0, pattern=[[1, P]], channel_multiplier=-1)
            e.affine_select(out=earlier, in_=earlier, compare_op=ALU.is_gt, fill=0.0,
                            base=0, pattern=[[1, NE], [-1, NE]], channel_multiplier=0).then_inc(s["mask0"], 1)

            e.iota(slot_row_i, pattern=[[1, P]], base=-P, channel_multiplier=0)
            e.iota(pad_tok_i.rearrange("p (b u) -> p b u", u=2), pattern=[[0, NB1 // 2], [P, 2]], base=T, channel_multiplier=1)
            e.iota(starts_i, pattern=[[P, NB1]], base=0, channel_multiplier=0)
            e.iota(tok_i.rearrange("p (k t) -> p k t", k=2), pattern=[[0, 2], [P, NT]], base=0,
                   channel_multiplier=1).then_inc(s["mask0"], 1)
            e.wait_ge(s["mask0"], 7)
            e.tensor_copy(slot_row, slot_row_i)
            e.tensor_copy(pad_tok, pad_tok_i[:, 0:NBLK])
            e.tensor_copy(starts, starts_i)
            e.tensor_copy(tok_col, tok_i).then_inc(s["mask0"], 1)

            e.wait_ge(s["tab_done"], 1)
            for u in range(2):
                e.wait_ge(x1_st[u], 16 * NT // 2)
                e.wait_ge(xn_st[u], 16 + 16 * NT // 2)
            e.wait_ge(s["pad_st"], 64)

            def gather(n, u):
                wait_apart(e, (s["m_tr"], n + 1))
                e.tensor_copy(tig[:, u, :], tab_tok[:, ds(n, 1)]).then_inc(s["tig_ready"], 1)
                wait_apart(e, (s["tig_ready"], n + 1))
                e.indirect_dma_start(xg[u], None, xn_rows,
                                     bass.IndirectOffsetOnAxis(tig[:, u, :], 0)).then_inc(xg_ld[u], 16)

            def scatter(n, u, k):
                if not isinstance(k, int) or k > 0:
                    wait_apart(e, (sc_done[u], 16 * k))
                e.tensor_copy(tis[:, u, :], tab_tok[:, ds(n, 1)]).then_inc(s["tis_ready"], 1)
                wait_apart(e, (s["tis_ready"], n + 1), (s["m_y"], n + 2))
                e.indirect_dma_start(out, bass.IndirectOffsetOnAxis(tis[:, u, :], 0), yb[u], None,
                                     compute_op=ALU.add).then_inc(sc_done[u], 16)

            for n in range(4):
                gather(n, n % 2)
            for n in range(2):
                gather(n + 4, n)
                scatter(n, n, 0)
            with e.Fori(1, NE // 2 - 2) as i:
                for u in range(2):
                    gather(2 * i + u + 4, u)
                    scatter(2 * i + u, u, i)
            for n in range(NE - 4, NE):
                scatter(n, n % 2, n // 2)
            for u in range(2):
                e.wait_ge(sc_done[u], 16 * NE // 2)
            e.wait_ge(s["ovf_ready"], 1)
            n_ov = e.value_load(ovf[0:1, MAXOV:MAXOV + 1], min_val=0, max_val=MAXOV)
            with e.If(n_ov > 0):
                with e.Fori(0, n_ov) as j:
                    gather(NE + j, 0)
                    scatter(NE + j, 0, NE // 2 + j)
                    wait_apart(e, (sc_done[0], 16 * (NE // 2 + j + 1)))

        @block.tensor
        def _(e):
            def mm(o, l, r, a=True, z=True):
                return nc.tensor.matmul(o, l, r, start=a, stop=z)

            e.wait_ge(s["early_ld"], 16 * N_EARLY)
            e.wait_ge(s["consts_done"], 1)
            nc.tensor.transpose(bank(0)[:, 0:20], rows, ident[0:20, 0:20]).then_inc(s["rows_tr"], 1)
            e.wait_ge(s["ada_done"], KT)
            for j in range(2 * KT):
                last = mm(bank(1)[:, j:j + 1], acc[:, 0, j * P:(j + 1) * P], onesf[:, 0:1])
            last.then_inc(s["mod1_ps"], 1)

            for t in range(NT):
                e.wait_ge(s["x_norm"], t + 1)
                e.wait_ge(s["h_evd"], t + 1)
                e.wait_ge(s["h_eva"], t + 1)
                for k in range(KT):
                    last = nc.tensor.transpose(bank(4 + 2 * (t % 2) + k // 4)[:, (k % 4) * P:(k % 4 + 1) * P],
                                               x_all[:, t, k * P:(k + 1) * P], ident[:, :])
                last.then_inc(s["x_tr"], 1)
            e.wait_ge(s["small_ld"], 16 * N_SMALL)
            e.wait_ge(s["h_evd"], 2 + NT)
            e.wait_ge(s["h_eva"], 2 + NT)

            def project(n):
                e.wait_ge(s["w_ld"], 16 * (n + 1))
                for t in range(NT):
                    e.wait_ge(s["proj_free"], n * NT + t + 1)
                    for k in range(KT):
                        last = mm(bank(t % 4), hT[:, k, t * P:(t + 1) * P], wring[:, n % 2, k, :],
                                  k == 0, k == KT - 1)
                    last.then_inc(s["proj_mm"], 1)

            with e.Fori(0, 3) as n:
                project(n)

            e.wait_ge(s["ada_done"], 3 * KT)
            e.wait_ge(s["proj_free"], 4 + 3 * NT)
            for j in range(KT):
                mm(bank(0)[:, j:j + 1], acc[:, 1, 1024 + j * P:1024 + (j + 1) * P], onesf[:, 0:1])
            for j in range(KT):
                mm(bank(0)[:, 8 + j:9 + j], acc[:, 2, j * P:(j + 1) * P], onesf[:, 0:1])
            for b, (g, o) in enumerate(((1, 0), (1, 512), (2, 1024), (2, 1536))):
                last = mm(bank(4 + b), onesf[:, :], acc[:, g, o:o + 512])
            last.then_inc(s["mods_ps"], 1)

            e.wait_ge(s["gates_done"], 1)
            for t in range(NT):
                e.wait_ge(s["rope_done"], t + 1)
                if t >= 2:
                    e.wait_ge(s["qT_done"], t - 1)
                    e.wait_ge(s["kT_done"], t - 1)
                for h in range(2 * NH):
                    last = nc.tensor.transpose(bank(4 + 2 * (t % 2) + h // NH)[:, (h % NH) * P:(h % NH + 1) * P],
                                               U[:, t, h * P:(h + 1) * P], ident[:, :])
                last.then_inc(s["qk_tr"], 1)
            e.wait_ge(s["mods_col"], 1)

            def glr(i):
                half = i // 4
                if i == 4:
                    e.wait_ge(s["glr_done"], 1)
                for k in (2 * (i % 4), 2 * (i % 4) + 1):
                    last = mm(bank(7)[0:RANK, :], wlr[:, k, :], hT[:, k, half * 512:(half + 1) * 512],
                              k == 0, k == KT - 1)
                if i % 4 == 3:
                    last.then_inc(s["glr_mm"], 1)

            def section_tile(n, i):
                e.wait_ge(s["w_ld"], 16 * (n + 1))
                e.wait_ge(s["proj_free"], 4 + n * NT + i)
                for k in range(KT):
                    last = mm(bank(7), hT[:, k, i * P:(i + 1) * P], wring[:, n % 2, k, :], k == 0, k == KT - 1)
                last.then_inc(s["proj_mm"], 1)

            def attend(h, between):
                def scores(i):
                    if i == 0:
                        e.wait_ge(s["head_staged"], h + 2)
                    e.wait_ge(s["exp_done"], h * NT + i + 1)
                    n = (i + 1) * P
                    for b in range((n + 511) // 512):
                        w = min(512, n - 512 * b)
                        diag = 512 * b + w == n
                        for c in range(2):
                            mm(bank(2 * c + b)[:, 0:w], qs[c * DK:(c + 1) * DK, i * P:(i + 1) * P],
                               ks[c * DK:(c + 1) * DK, 512 * b:512 * b + w], True, not diag)
                    for c in range(2):
                        last = mm(bank(2 * c + i // 4)[:, (i % 4) * P:(i % 4 + 1) * P],
                                  identb[:, :], causal_neg[:, :], False, True)
                    last.then_inc(s["scores_ready"], 1)

                def turn(i):
                    e.wait_ge(s["att_a"], h * NT + i + 3)
                    e.wait_ge(s["aT_done"], h * NT + i + 1)
                    for j in range(i + 1):
                        last = nc.tensor.transpose(bank(4 + j // 4)[:, (j % 4) * P:(j % 4 + 1) * P],
                                                   attn[i % 2][:, j * P:(j + 1) * P], ident[:, :])
                    last.then_inc(s["att_tr"], 1)

                def weigh(i):
                    e.wait_ge(s["aT_done"], h * NT + i + 2)
                    e.wait_ge(s["att_o_done"], h * NT + i + 2)
                    for j in range(i + 1):
                        last = mm(bank(6)[:, 0:DV], attnT[i % 2][:, j * P:(j + 1) * P],
                                  U[:, j, ds(1024 + h * DV, DV)], j == 0, j == i)
                    last.then_inc(s["att_o"], 1)

                scores(0)
                for i in range(NT):
                    if i + 1 < NT:
                        scores(i + 1)
                    between(i)
                    turn(i)
                    if i >= 1:
                        weigh(i - 1)
                weigh(NT - 1)

            attend(0, glr)
            e.wait_ge(s["glr_done"], 2)
            with e.Fori(1, NH) as h:
                attend(h, lambda i: section_tile(h + 2, i))
            for t in range(NT):
                last = mm(bank(0, 4)[:, t * 256:(t + 1) * 256], alrT[:, t * P:(t + 1) * P], aup)
            last.then_inc(s["z_mm"], 1)

            def early_gate(f, x, half, b):
                e.wait_ge(gw_ld[1 - f], 64)
                for k in range(KT):
                    last = mm(bank(b), gw[1 - f][:, 8 * x + k, :], hT[:, k, ds(half * 512, 512)], k == 0, k == KT - 1)
                last.then_inc(s["early_mm"], 1)

            e.wait_ge(s["att_o_done"], 2 + NH * NT)
            early_gate(1, 0, 0, 6)
            e.wait_ge(s["proj_free"], 4 + 6 * NT)
            early_gate(1, 1, 0, 7)
            for t in range(NT):
                e.wait_ge(s["ob_norm"], t + 1)
                if t >= 2:
                    e.wait_ge(s["obT_done"], t - 1)
                for h in range(NH):
                    last = nc.tensor.transpose(bank(4 + t % 2)[:, h * P:(h + 1) * P], o_att[:, h, t, :], ident[:, :])
                last.then_inc(s["ob_tr"], 1)
            e.wait_ge(s["g_done"], 1)
            e.wait_ge(s["obT_done"], NT)
            e.wait_ge(s["early_sig"], 2)
            for b in range(4):
                mm(bank(b), tri[:, :], sp[:, 512 * b:512 * (b + 1)])
            for b in range(4):
                last = mm(bank(4 + b), suf[:, :], sp[:, 512 * b:512 * (b + 1)])
            last.then_inc(s["cum_mm"], 1)
            e.wait_ge(s["eb_done"], 1)
            for t in range(NT):
                for pr in range(2):
                    last = mm(bank(7)[:, t * 4 + pr * 2:t * 4 + pr * 2 + 2],
                              sp[:, t * 256 + pr * P:t * 256 + (pr + 1) * P], blk[:, 0:P:CH])
            last.then_inc(s["dec_mm"], 1)

            def gla_o(t, u):
                e.wait_ge(s["gla_attS"], t + 1)
                e.wait_ge(s["gla_mid"], t + 1)
                e.wait_ge(s["gla_o_done"], t + 1)
                for hd in range(NH):
                    r0, pr = DK * (hd % 2), hd // 2
                    o = bank(5 + hd % 2)[:, pr * DV:(pr + 1) * DV]
                    mm(o, attS[u][:, hd, :], vcp[u][:, hd * DV:(hd + 1) * DV], True, False)
                    mm(o[0:CH, :], qkT[u][r0:r0 + DK, pr, 0:CH], S_in[u][r0:r0 + DK, pr, :], False, True)
                    last = mm(o[CH:P, :], qkT[u][r0:r0 + DK, pr, CH:P], S_mid[u][r0:r0 + DK, pr, :], False, True)
                last.then_inc(s["gla_o"], 1)

            def gla_first(t, u):
                e.wait_ge(s["gla_in"], t + 1)
                e.wait_ge(s["gla_qkT"], t + 1)
                for x in range(4):
                    src = (qin, kin)[x // 2][u][:, (x % 2) * P:(x % 2 + 1) * P]
                    last = nc.tensor.transpose(bank(0)[:, x * P:(x + 1) * P], src, ident[:, :])
                last.then_inc(s["gla_tr"], 1)
                wait_apart(e, (s["gla_vcopy"], t + 1), (s["gla_out_state"], t + 1))
                for c in range(2):
                    for hd in range(NH):
                        r0, pr = DK * (hd % 2), hd // 2
                        last = mm(bank(3 + c)[r0:r0 + DK, pr * DV:(pr + 1) * DV],
                                  kdc[u][c * CH:(c + 1) * CH, hd * DK:(hd + 1) * DK],
                                  vcp[u][c * CH:(c + 1) * CH, hd * DV:(hd + 1) * DV])
                last.then_inc(s["gla_sc"], 1)

            def gla_att(t, u):
                e.wait_ge(s["gla_qkT"], t + 2)
                for hd in range(NH):
                    r0, pr = DK * (hd % 2), hd // 2
                    last = mm(bank(1 + hd % 2)[:, pr * P:(pr + 1) * P], qkT[u][r0:r0 + DK, 2 + pr, :],
                              qkT[u][r0:r0 + DK, pr, :])
                last.then_inc(s["gla_att"], 1)

            early_gate(1, 0, 1, 6)
            e.wait_ge(s["dec_done"], 1)
            e.wait_ge(s["gla_zero"], 1)
            gla_first(0, 0)
            early_gate(1, 1, 1, 7)
            gla_att(0, 0)
            e.wait_ge(s["early_sig"], 3)

            def gla_pair(i, gates):
                for u in range(2):
                    t = 2 * i + u
                    gla_first(t + 1, 1 - u)
                    if gates:
                        e.wait_ge(s["early_sig"], t + 4)
                        early_gate(0, u, i, 7)
                    gla_o(t, u)
                    gla_att(t + 1, 1 - u)

            with e.Fori(0, 2) as i:
                gla_pair(i, True)
            with e.Fori(2, NT // 2 - 1) as i:
                gla_pair(i, False)
            gla_first(NT - 1, 1)
            gla_o(NT - 2, 0)
            gla_att(NT - 1, 1)
            gla_o(NT - 1, 1)

            def early_branch(f, half, src, k0, b):
                for k in range(4):
                    last = mm(bank(b), gw[1 - f][:, k0 + k, :], src[:, k, half * 512:(half + 1) * 512], k == 0, k == 3)
                return last

            e.wait_ge(s["gla_attS"], NT)
            e.wait_ge(s["gla_out_state"], 1 + NT)
            e.wait_ge(s["early_sig"], 8)
            e.wait_ge(s["gla_o_done"], 1 + NT)
            for f in (1, 0):
                for half in range(2):
                    early_branch(f, half, obT, 20, 4 * half + 3 - 2 * f)
            for t in range(NT):
                e.wait_ge(s["oa_norm"], t + 1)
                if t >= 2:
                    e.wait_ge(s["oaT_done"], t - 1)
                for h in range(NH):
                    last = nc.tensor.transpose(bank(4 * (t % 2))[:, h * P:(h + 1) * P],
                                               U[:, t, 1024 + h * P:1024 + (h + 1) * P], ident[:, :])
                last.then_inc(s["oa_tr"], 1)
            e.wait_ge(s["oaT_done"], NT)
            for f in (1, 0):
                for half in range(2):
                    early_branch(f, half, oaT, 16, 4 * half + 2 - 2 * f).then_inc(s["g_mm"], 1)

            with e.Fori(1, KT // 2) as i:
                for u in range(2):
                    e.wait_ge(gw_ld[u], 64 * (i + 1))
                    for half in range(2):
                        e.wait_ge(s["g_free"], 2 * (2 * i + u) + half + 3)
                        tok = slice(half * 512, (half + 1) * 512)
                        for b, (k0, nk, src) in enumerate(((0, 8, hT), (8, 8, hT), (16, 4, oaT), (20, 4, obT))):
                            for k in range(nk):
                                last = mm(bank(4 * half + b), gw[u][:, k0 + k, :], src[:, k, tok],
                                          k == 0, k == nk - 1)
                        last.then_inc(s["g_mm"], 1)

            e.wait_ge(s["wout_ld"], 16)
            e.wait_ge(s["g_sig"], 2 * KT - 4)
            for half in range(2):
                for k in range(KT):
                    if half == 0 and k == KT - 1:
                        e.wait_ge(s["g_free"], 4 + 2 * KT)
                    last = mm(bank(half), mT[:, k, 0:P], wout[:, k, half * 512:(half + 1) * 512], k == 0, k == KT - 1)
            last.then_inc(s["mo_mm"], 1)

            def out_proj(t, u, half):
                if half == 0:
                    e.wait_ge(s["ms_ready"], t)
                    e.wait_ge(s["mo_gated"], t + 1)
                for k in range(KT):
                    last = mm(bank(2 * u + half), ms[u][:, k, :], wout[:, k, half * 512:(half + 1) * 512],
                              k == 0, k == KT - 1)
                if half == 1:
                    last.then_inc(s["mo_mm"], 1)

            def turn_h2(t, u):
                e.wait_ge(s["xn2_ready"], t + 1)
                e.wait_ge(s["h2_evd"], t + 1)
                e.wait_ge(s["h2_eva"], t + 1)
                for k in range(KT):
                    last = nc.tensor.transpose(bank(4 + k // 4)[:, (k % 4) * P:(k % 4 + 1) * P],
                                               xn[u][:, k * P:(k + 1) * P], ident[:, :])
                last.then_inc(s["h2_tr"], 1)

            def route(t, u):
                e.wait_ge(s["h2_evd"], t + 2)
                e.wait_ge(s["h2_eva"], t + 2)
                e.wait_ge(s["rt_done"], t + 1)
                for k in range(KT):
                    last = mm(bank(6)[:, 0:NR], h2T[u][:, k, :], wr[:, k, :], k == 0, k == KT - 1)
                last.then_inc(s["rt_mm"], 1)

            def step(t, u):
                out_proj(t + 1, 1 - u, 0)
                turn_h2(t, u)
                out_proj(t + 1, 1 - u, 1)
                route(t, u)

            with e.Fori(0, NT // 2 - 1) as i:
                for u in range(2):
                    step(2 * i + u, u)
            step(NT - 2, 0)
            turn_h2(NT - 1, 1)
            route(NT - 1, 1)

            e.wait_ge(s["rt_m"], 1)
            e.wait_ge(s["mask0"], 6)
            mm(bank(0)[:, 0:NT * NE], before, choice_b[:, 0:NT, :].rearrange("p t e -> p (t e)"), True, False)
            mm(bank(0)[:, 0:NT * NE], onesb, choice_b[:, NT:2 * NT, :].rearrange("p t e -> p (t e)"), False, True)
            mm(bank(1)[:, 0:NE], onesb, choice_b[:, 2 * NT, :]).then_inc(s["rt_sums_mm"], 1)
            for c in range(2 * NT):
                e.wait_ge(s["slots_in"], c // NT + 1)
                last = mm(bank(2)[:, 0:3 * NBLK], d1[:, c, :], d2[:, c, :, :].rearrange("p x b -> p (x b)"),
                          c == 0, c == 2 * NT - 1)
            last.then_inc(s["rt_sums_mm"], 1)

            def rows_in(n, u, k):
                e.wait_ge(xg_ld[u], 16 * (k + 1))
                e.wait_ge(s["m_evd"], n + 1)
                e.wait_ge(s["m_eva"], n + 1)
                for j in range(KT):
                    last = nc.tensor.transpose(bank(j // 4)[:, (j % 4) * P:(j % 4 + 1) * P],
                                               xg[u][:, j * P:(j + 1) * P], ident[:, :])
                last.then_inc(s["m_tr"], 1)

            def up(n, u, k):
                e.wait_ge(s["m_evd"], n + 2)
                e.wait_ge(s["m_eva"], n + 2)
                e.wait_ge(w13_ld[u], 32 * (k + 1))
                e.wait_ge(s["m_hh"], n + 1)
                for w in range(2):
                    for j in range(KT):
                        last = mm(bank(2 + w), xT[u][:, j, :], w13[u][:, w, j, :], j == 0, j == KT - 1)
                last.then_inc(s["m1_mm"], 1)

            def turn_hh(n):
                e.wait_ge(s["m_hh"], n + 2)
                e.wait_ge(s["m_hhT"], n + 1)
                for j in range(4):
                    last = nc.tensor.transpose(bank(4)[:, j * P:(j + 1) * P], hh[:, j * P:(j + 1) * P], ident[:, :])
                last.then_inc(s["m2_tr"], 1)

            def down(n, u, k):
                e.wait_ge(s["m_hhT"], n + 2)
                e.wait_ge(w2_ld[u], 16 * (k + 1))
                e.wait_ge(s["m_y"], n + 1)
                for half in range(2):
                    for j in range(4):
                        last = mm(bank(6 + half), hhT[:, j, :], w2b[u][:, j, half * 512:(half + 1) * 512],
                                  j == 0, j == 3)
                last.then_inc(s["m2_mm"], 1)

            rows_in(0, 0, 0)
            up(0, 0, 0)
            rows_in(1, 1, 0)
            with e.Fori(0, NE // 2 - 1) as i:
                for u in (1, 0):
                    n = 2 * i + 2 - u
                    turn_hh(n - 1)
                    up(n, u, i + 1 - u)
                    rows_in(n + 1, 1 - u, i + 1)
                    down(n - 1, 1 - u, i)
            kl = NE // 2 - 1
            turn_hh(NE - 2)
            up(NE - 1, 1, kl)
            down(NE - 2, 0, kl)
            turn_hh(NE - 1)
            down(NE - 1, 1, kl)
            e.wait_ge(s["ovf_ready"], 1)
            n_ov = e.value_load(ovf[0:1, MAXOV:MAXOV + 1], min_val=0, max_val=MAXOV)
            with e.If(n_ov > 0):
                with e.Fori(0, n_ov) as j:
                    n, k = NE + j, NE // 2 + j
                    rows_in(n, 0, k)
                    up(n, 0, k)
                    turn_hh(n)
                    down(n, 0, k)

        @block.scalar
        def _(e):
            def act(o, i, f, **kw):
                return nc.scalar.activation(o, i, f, **kw)

            for sem, n in ((s["h_eva"], 2), (s["proj_free"], 4), (s["exp_done"], 1), (s["aT_done"], 1), (s["gla_qkT"], 1),
                           (s["gla_o_done"], 1), (s["h2_eva"], 1), (s["m_eva"], 1), (s["m_hhT"], 1), (s["scores_ready"], 1),
                           (s["m2_mm"], 1)):
                e.sem_inc(sem, n)
            e.wait_ge(s["c_ld"], 16)
            act(cact[:, 1, :], cact[:, 0, :], ACT.Exp, scale=-1.0).then_inc(s["cact_e"], 1)

            for g in range(2):
                e.wait_ge(x_ld[g], 16)
                if g == 1:
                    e.wait_ge(s["x_sq"], 1)
                for j in range(4):
                    t = 4 * g + j
                    last = act(WK[:, 1024 * j:1024 * (j + 1)], x_all[:, t, :], ACT.Square, accum_out=xstat[:, 0, t:t + 1])
                last.then_inc(s["x_sq"], 1)
                e.wait_ge(s["x_sq"], g + 1)
                act(xstat[:, 1, 4 * g:4 * g + 4], xstat[:, 0, 4 * g:4 * g + 4], ACT.Sqrt, scale=1.0 / D,
                    bias=EPS).then_inc(s["x_sd"], 1)
            e.wait_ge(s["mod1_done"], 1)
            for t in range(NT):
                e.wait_ge(s["x_tr"], t + 1)
                for k in range(4):
                    last = act(hT[:, 4 + k, t * P:(t + 1) * P], bank(5 + 2 * (t % 2))[:, k * P:(k + 1) * P], ACT.Identity,
                               scale=A1[:, 4 + k:5 + k], bias=S1[:, 4 + k:5 + k])
                last.then_inc(s["h_eva"], 1)
            e.wait_ge(s["lam_p"], 1)
            act(lam[:, 2:4], lam[:, 0:2], ACT.Exp).then_inc(s["lam_e"], 1)
            e.wait_ge(s["rope_arg"], 1)
            act(sincos[:, 0].rearrange("p t f -> p (t f)"), ang[:, 3, :], ACT.Sin)
            act(sincos[:, 1].rearrange("p t f -> p (t f)"), ang[:, 2, :], ACT.Sin).then_inc(s["rope_sin"], 1)

            def read_section(n, col):
                for t in range(NT):
                    e.wait_ge(s["proj_mm"], n * NT + t + 1)
                    act(U[:, t, ds(col, HW)], bank(t % 4), ACT.Copy).then_inc(s["proj_free"], 1)

            with e.Fori(0, 2) as n:
                read_section(n, n * HW)
            with e.Fori(0, NT // 2) as i:
                for u in range(2):
                    t = 2 * i + u
                    e.wait_ge(s["proj_free"], 4 + NT + t + 1)
                    e.wait_ge(s["qk_sum"], t + 1)
                    act(junk[u], U[:, t, 0:1024], ACT.Square).then_inc(s["qk_sq"], 1)
            e.wait_ge(s["qk_sum"], 2 + NT)
            act(ssqk, ssqk, ACT.Sqrt, scale=1.0 / DK, bias=EPS).then_inc(s["qk_sd"], 1)
            read_section(2, 2 * HW)
            e.wait_ge(s["mods_ps"], 1)
            for b in range(4):
                last = act(gate[:, b // 2, (b % 2) * 512:(b % 2 + 1) * 512], bank(4 + b), ACT.Copy)
            last.then_inc(s["gates_done"], 1)
            for t in range(NT):
                e.wait_ge(s["qk_tr"], t + 1)
                act(qT[:, :, t * P:(t + 1) * P], bank(4 + 2 * (t % 2)).rearrange("p (h t) -> p h t", h=NH),
                    ACT.Copy, scale=gcols[:, 16:17]).then_inc(s["qT_done"], 1)

            e.wait_ge(s["qT_done"], NT)
            act(qs, qT[:, 0, :], ACT.Copy).then_inc(s["head_staged"], 1)

            def attend(h, between):
                def exps(i):
                    e.wait_ge(s["nmax_ready"], h * NT + i + 1)
                    e.wait_ge(s["att_a"], h * NT + i + 1)
                    for c in range(2):
                        last = act(E[:, i % 2, c, 0:(i + 1) * P], bank(2 * c, 2)[:, 0:(i + 1) * P], ACT.Exp,
                                   scale=DK ** -0.5, bias=att_nm[:, i % 2, c:c + 1],
                                   accum_out=att_sum[:, i % 2, c:c + 1])
                    last.then_inc(s["exp_done"], 1)

                exps(0)
                for i in range(NT):
                    if i + 1 < NT:
                        exps(i + 1)
                    e.wait_ge(s["att_tr"], h * NT + i + 3)
                    e.wait_ge(s["att_o"], h * NT + i + 1)
                    act(attnT[i % 2][:, 0:(i + 1) * P], bank(4, 2)[:, 0:(i + 1) * P], ACT.Copy).then_inc(s["aT_done"], 1)
                    between(i)

            def glr_read(i):
                if i % 4 == 3:
                    e.wait_ge(s["glr_mm"], i // 4 + 1)
                    e.wait_ge(s["alr_ones"], 1)
                    act(alrT[0:RANK, (i // 4) * 512:(i // 4 + 1) * 512], bank(7)[0:RANK, :], ACT.Copy).then_inc(s["glr_done"], 1)

            def section_read(n, i, dst):
                e.wait_ge(s["proj_mm"], n * NT + i + 1)
                act(dst, bank(7), ACT.Copy).then_inc(s["proj_free"], 1)

            def ob_square(h, i, unused):
                return act(unused[:, DV * i:DV * (i + 1)], qT[:, ds(h, 1), i * P:(i + 1) * P].rearrange("p o d -> p (o d)"),
                           ACT.Square, accum_out=sso[:, 0, ds(h * NT + i, 1)])

            def section_and_square(h, i, dst):
                section_read(h + 2, i, dst)
                e.wait_ge(s["att_o_done"], h * NT + i - NT + 3)
                ob_square(h - 1, i, junk[1])

            attend(0, glr_read)
            with e.Fori(1, NH - 1) as h:
                attend(h, lambda i: section_and_square(h, i, U[:, i, ds(1024 - 512 * h, HW)]))
            attend(NH - 1, lambda i: section_and_square(NH - 1, i, gv_tmp[:, i, :]))

            e.wait_ge(s["att_o_done"], 2 + NH * NT)
            for i in range(NT):
                last = ob_square(NH - 1, i, attn[0])
            last.then_inc(s["ob_sq"], 1)
            e.wait_ge(s["ob_sq"], 1)
            act(sso[:, 0, :], sso[:, 0, :], ACT.Sqrt, scale=1.0 / DV, bias=EPS).then_inc(s["out_sd"], 1)

            e.wait_ge(s["z_mm"], 1)
            act(sp, bank(0, 4), ACT.Abs).then_inc(s["z_step"], 1)
            e.wait_ge(s["z_step"], 1)
            act(sp, sp, ACT.Exp, scale=-1.0).then_inc(s["z_step"], 1)
            e.wait_ge(s["z_step"], 2)
            act(sp, sp, ACT.Ln, bias=1.0).then_inc(s["z_step"], 1)

            def early_sigmoid(n, dst, b):
                e.wait_ge(s["early_mm"], n + 1)
                act(dst, bank(b), ACT.Sigmoid).then_inc(s["early_sig"], 1)

            early_sigmoid(0, early[1][0][0], 6)
            early_sigmoid(1, early[1][1][0], 7)
            for t in range(NT):
                e.wait_ge(s["ob_tr"], t + 1)
                act(obT[:, :, t * P:(t + 1) * P], bank(4 + t % 2).rearrange("p (h t) -> p h t", h=NH),
                    ACT.Copy, scale=gcols[:, 19:20]).then_inc(s["obT_done"], 1)
            e.wait_ge(s["cum_mm"], 1)
            e.wait_ge(s["gv_moved"], 1)
            act(R2[:, 6144:8192], bank(4, 4), ACT.Exp).then_inc(s["eb_done"], 1)
            act(R2[:, 2048:4096], bank(0, 4), ACT.Exp).then_inc(s["eb_done"], 1)
            act(R2[:, 4096:6144], bank(0, 4), ACT.Exp, scale=-1.0).then_inc(s["eb_done"], 1)
            e.wait_ge(s["dec_mm"], 1)
            act(dec[:, :], bank(7)[:, 0:4 * NT], ACT.Exp).then_inc(s["dec_done"], 1)

            def gla_read(t, u):
                e.wait_ge(s["gla_tr"], t + 1)
                e.wait_ge(s["gla_o"], t + 1)
                act(qkT[u].rearrange("p x t -> p (x t)"), bank(0), ACT.Copy).then_inc(s["gla_qkT"], 1)

            def gla_out(t):
                e.wait_ge(s["gla_o"], t + 3)
                for par in range(2):
                    last = act(U[:, t, 1024:1536].rearrange("p (x y v) -> p x y v", x=2, y=2)[:, :, par, :],
                               bank(5 + par)[:, 0:256].rearrange("p (x v) -> p x v", x=2), ACT.Copy)
                last.then_inc(s["gla_o_done"], 1)

            early_sigmoid(2, early[1][0][1], 6)
            gla_read(0, 0)
            early_sigmoid(3, early[1][1][1], 7)
            with e.Fori(0, 2) as i:
                for u in range(2):
                    gla_read(2 * i + u + 1, 1 - u)
                    early_sigmoid(2 * i + u + 4, (WK[:, ds(2304 + 512 * i, 512)], R2[:, ds(512 * i, 512)])[u], 7)
                    gla_out(2 * i + u)
            with e.Fori(2, NT // 2 - 1) as i:
                for u in range(2):
                    gla_read(2 * i + u + 1, 1 - u)
                    gla_out(2 * i + u)
            gla_read(NT - 1, 1)
            gla_out(NT - 2)
            gla_out(NT - 1)

            e.wait_ge(s["gla_o_done"], 1 + NT)
            with e.Fori(0, NT // 2) as i:
                for u in range(2):
                    e.wait_ge(s["oa_sum"], 2 * i + u + 1)
                    act(R4[:, HW * u:HW * (u + 1)], U[:, 2 * i + u, 1024:1536], ACT.Square).then_inc(s["oa_sq"], 1)
            e.wait_ge(s["oa_sum"], 2 + NT)
            act(sso[:, 1, :], sso[:, 1, :], ACT.Sqrt, scale=1.0 / DV, bias=EPS).then_inc(s["out_sd"], 1)
            act(U[:, :, 0:HW], U[:, :, 0:HW], ACT.Silu).then_inc(s["oa_silu"], 1)
            for t in range(NT):
                e.wait_ge(s["oa_tr"], t + 1)
                act(oaT[:, :, t * P:(t + 1) * P], bank(4 * (t % 2)).rearrange("p (h t) -> p h t", h=NH),
                    ACT.Copy, scale=gcols[:, 18:19]).then_inc(s["oaT_done"], 1)

            with e.Fori(4, 2 * KT, 2) as n:
                for half in range(2):
                    e.wait_ge(s["g_mm"], n + half + 1)
                    e.wait_ge(s["g_free"], n + half + 3)
                    act(sig[:, 2 * half, :], bank(4 * half), ACT.Sigmoid)
                    act(sig[:, 2 * half + 1, :], bank(4 * half + 1), ACT.Sigmoid).then_inc(s["g_sig"], 1)

            with e.Fori(0, NT // 2) as i:
                for u in range(2):
                    t = 2 * i + u
                    e.wait_ge(s["x1_ready"], t + 1)
                    e.wait_ge(s["rt_mm"], t + 1)
                    act(h2T[u].rearrange("p k t -> p (k t)"), xh[u], ACT.Square,
                        accum_out=stat[:, 2, u:u + 1]).then_inc(s["x1_sq"], 1)
                    e.wait_ge(s["x1_sq"], t + 1)
                    act(stat[:, 3, u:u + 1], stat[:, 2, u:u + 1], ACT.Sqrt, scale=1.0 / D, bias=EPS).then_inc(s["x1_sd"], 1)
                    e.wait_ge(s["x1_rs"], t + 1)
                    act(xn[u], xh[u], ACT.Copy, scale=stat[:, 2, u:u + 1]).then_inc(s["xn2_ready"], 1)
                    e.wait_ge(s["h2_tr"], t + 3)
                    for k in range(4):
                        last = act(h2T[u][:, 4 + k, :], bank(5)[:, k * P:(k + 1) * P], ACT.Identity,
                                   scale=A2[:, 4 + k:5 + k], bias=S2[:, 4 + k:5 + k])
                    last.then_inc(s["h2_eva"], 1)

            e.wait_ge(s["rt_diff"], 1)
            act(rt_gd, rt_gd, ACT.Exp).then_inc(s["rt_exp"], 1)
            e.wait_ge(s["rt_diff"], 2)
            act(rt_d[:, 1, :], rt_d[:, 0, :], ACT.Exp).then_inc(s["rt_exp"], 1)

            def rows_read(n, u):
                e.wait_ge(s["m_tr"], n + 3)
                for k in range(4):
                    last = act(xT[u][:, 4 + k, :], bank(1)[:, k * P:(k + 1) * P], ACT.Identity,
                               scale=A2[:, 4 + k:5 + k], bias=S2[:, 4 + k:5 + k])
                last.then_inc(s["m_eva"], 1)

            def silu(n):
                e.wait_ge(s["m1_mm"], n + 1)
                e.wait_ge(s["m_hh"], n + 1)
                act(sg, bank(2), ACT.Silu).then_inc(s["m_silu"], 1)

            def hh_read(n):
                e.wait_ge(s["m2_tr"], n + 2)
                e.wait_ge(s["m2_mm"], n + 1)
                act(hhT.rearrange("p k t -> p (k t)"), bank(4), ACT.Copy).then_inc(s["m_hhT"], 1)

            rows_read(0, 0)
            silu(0)
            rows_read(1, 1)
            with e.Fori(0, NE // 2 - 1) as i:
                for u in (1, 0):
                    n = 2 * i + 2 - u
                    hh_read(n - 1)
                    silu(n)
                    rows_read(n + 1, 1 - u)
            hh_read(NE - 2)
            silu(NE - 1)
            hh_read(NE - 1)
            e.wait_ge(s["ovf_ready"], 1)
            n_ov = e.value_load(ovf[0:1, MAXOV:MAXOV + 1], min_val=0, max_val=MAXOV)
            with e.If(n_ov > 0):
                with e.Fori(0, n_ov) as j:
                    rows_read(NE + j, 0)
                    silu(NE + j)
                    hh_read(NE + j)

        @block.vector
        def _(e):
            v = nc.vector

            def tt(o, a, b, op):
                return v.tensor_tensor(o, a, b, op)

            def tsc(o, a, c1, op0, c2=None, op1=None):
                if op1 is None:
                    return v.tensor_scalar(o, a, c1, None, op0)
                return v.tensor_scalar(o, a, c1, c2, op0, op1)

            def stt(o, a, c, b, op0, op1):
                return v.scalar_tensor_tensor(out=o, in0=a, scalar=c, in1=b, op0=op0, op1=op1)

            def spread(a, shape):
                return a.to_broadcast(shape)

            for sem, n in ((s["h_evd"], 2), (s["qk_sum"], 2), (s["att_a"], 2), (s["att_o"], 2), (s["att_tr"], 2), (s["att_o_done"], 2),
                           (s["oa_sum"], 2), (s["gla_sc"], 2), (s["gla_o"], 2), (s["gla_out_state"], 1),
                           (s["g_free"], 4), (s["mo_mm"], 2), (s["mo_gated"], 2), (s["h2_tr"], 2), (s["h2_evd"], 1), (s["rt_mm"], 2),
                           (s["rt_done"], 1), (s["m_tr"], 2), (s["m_evd"], 1), (s["m_hh"], 1), (s["m2_tr"], 1),
                           (s["m_y"], 1), (xn_st[0], 16), (xn_st[1], 16)):
                e.sem_inc(sem, n)

            e.wait_ge(s["cact_e"], 1)
            tsc(cact[:, 2, :], cact[:, 1, :], 1.0, ALU.add).then_inc(s["cact_1"], 1)
            e.wait_ge(s["cact_1"], 1)
            v.reciprocal(cact[:, 1, :], cact[:, 2, :]).then_inc(s["cact_1"], 1)
            e.wait_ge(s["cact_1"], 2)
            tt(cact[:, 3, :], cact[:, 0, :], cact[:, 1, :], ALU.mult).then_inc(s["cact_1"], 1)
            e.wait_ge(s["rows_tr"], 1)
            v.tensor_copy(gcols[:, 0:19], bank(0)[:, 0:19])
            tsc(gcols[:, 19:20], bank(0)[:, 19:20], 1.0 - LAMBDA_INIT, ALU.mult).then_inc(s["rows_cols"], 1)

            def ada(g, j):
                n = g * KT + j
                e.wait_ge(ada_ld[j % 4], 16 * (2 * g + j // 4 + 1))
                e.wait_ge(s["ada_done"], n)
                stt(acc[:, g, :], aw[j % 4], cact[:, 3, j:j + 1], acc[:, g, :], ALU.mult, ALU.add).then_inc(s["ada_done"], 1)

            e.wait_ge(s["early_ld"], 16 * N_EARLY)
            e.wait_ge(s["fills_done"], 2)
            e.wait_ge(s["cact_1"], 3)
            for j in range(KT):
                ada(0, j)

            def normalise(g):
                e.wait_ge(s["x_sd"], g + 1)
                v.reciprocal(xstat[:, 0, 4 * g:4 * g + 4], xstat[:, 1, 4 * g:4 * g + 4]).then_inc(s["x_rs"], 1)
                e.wait_ge(s["x_rs"], g + 1)
                for t in range(4 * g, 4 * g + 4):
                    tsc(x_all[:, t, :], x_all[:, t, :], xstat[:, 0, t:t + 1], ALU.mult).then_inc(s["x_norm"], 1)

            def modulate(t):
                e.wait_ge(s["x_tr"], t + 1)
                for k in range(4):
                    last = tsc(hT[:, k, t * P:(t + 1) * P], bank(4 + 2 * (t % 2))[:, k * P:(k + 1) * P],
                               A1[:, k:k + 1], ALU.mult, S1[:, k:k + 1], ALU.add)
                last.then_inc(s["h_evd"], 1)

            normalise(0)
            e.wait_ge(s["mod1_ps"], 1)
            e.wait_ge(s["rows_cols"], 1)
            v.tensor_copy(S1[:, :], bank(1)[:, 0:KT])
            stt(A1[:, :], bank(1)[:, KT:2 * KT], 1.0, gcols[:, 0:KT], ALU.add, ALU.mult).then_inc(s["mod1_done"], 1)
            e.wait_ge(s["mod1_done"], 1)
            modulate(0)
            modulate(1)
            normalise(1)
            for t in range(2, NT):
                modulate(t)

            e.wait_ge(s["small_ld"], 16 * N_SMALL)
            for j in range(2):
                last = v.tensor_tensor_reduce(out=junk[1][:, j * DK:(j + 1) * DK], in0=lq[:, 2 * j, :], in1=lq[:, 2 * j + 1, :],
                                              scale=1.0, scalar=0.0, op0=ALU.mult, op1=ALU.add,
                                              accum_out=lam[:, j:j + 1])
            last.then_inc(s["lam_p"], 1)
            e.wait_ge(s["lam_e"], 1)
            tt(lam[:, 5:6], lam[:, 3:4], lam[:, 2:3], ALU.subtract).then_inc(s["lam_done"], 1)
            e.wait_ge(s["lam_done"], 1)
            tsc(lam[:, 4:5], lam[:, 5:6], -LAMBDA_INIT, ALU.add).then_inc(s["lam_done"], 1)

            n_rope = [0]

            def rope(ins):
                n_rope[0] += 1
                ins.then_inc(s["rope_step"], 1)
                e.wait_ge(s["rope_step"], n_rope[0])

            def wrapped(x, tmp):
                for op, lim, turn in ((ALU.is_gt, PI, -2 * np.pi), (ALU.is_lt, -PI, 2 * np.pi)):
                    rope(tsc(tmp, x, lim, op, float(turn), ALU.mult))
                    rope(tt(x, x, tmp, ALU.add))
                rope(tsc(x, x, PI, ALU.min, -PI, ALU.max))

            rope(v.tensor_copy(posf[:, :], pos[:, :]))
            angv = ang[:, 0, :].rearrange("p (t f) -> p t f", f=HALF)
            for f in range(HALF):
                last = tsc(angv[:, :, f], posf[:, :], INV_FREQ[f], ALU.mult)
            rope(last)
            rope(tsc(angi, ang[:, 0, :], float(1 / (2 * np.pi)), ALU.mult))
            rope(v.tensor_copy(ang[:, 1, :], angi))
            rope(stt(ang[:, 2, :], ang[:, 1, :], -TWO_PI_HI, ang[:, 0, :], ALU.mult, ALU.add))
            rope(stt(ang[:, 2, :], ang[:, 1, :], -TWO_PI_LO, ang[:, 2, :], ALU.mult, ALU.add))
            wrapped(ang[:, 2, :], ang[:, 1, :])
            rope(tsc(ang[:, 3, :], ang[:, 2, :], float(np.pi / 2), ALU.add))
            wrapped(ang[:, 3, :], ang[:, 1, :])
            e.sem_inc(s["rope_arg"], 1)

            with e.Fori(1, 3) as g:
                for j in range(KT):
                    ada(g, j)

            with e.Fori(0, NT // 2) as i:
                for u in range(2):
                    t = 2 * i + u
                    e.wait_ge(s["qk_sq"], t + 1)
                    v.tensor_reduce(ssqk[:, ds(t * 16, 16)], junk[u].rearrange("p (c d) -> p c d", d=DK),
                                    AX.X, ALU.add).then_inc(s["qk_sum"], 1)
            e.wait_ge(s["qk_sd"], 1)
            v.reciprocal(rqk.rearrange("p t c -> p (t c)"), ssqk).then_inc(s["qk_rs"], 1)
            e.wait_ge(s["qk_rs"], 1)
            e.wait_ge(s["rope_sin"], 1)
            pre = ropeb[:, 0:256]
            x1, x2 = (pre.rearrange("p (c d) -> p c d", d=ROPE)[:, :, HALF * j:HALF * (j + 1)] for j in range(2))
            prod = [ropeb[:, 256 + 128 * j:384 + 128 * j].rearrange("p (c d) -> p c d", d=HALF) for j in range(4)]
            with e.Fori(0, NT) as t:
                qk = U[:, t, 0:1024].rearrange("p (c d) -> p c d", d=DK)
                tt(qk, qk, spread(rqk[:, t, :].rearrange("p (c o) -> p c o", o=1), [P, 16, DK]), ALU.mult).then_inc(s["qk_scaled"], 1)
                e.wait_ge(s["qk_scaled"], t + 1)
                tt(pre.rearrange("p (x h d) -> p x h d", x=2, h=8),
                   U[:, t, 0:1024].rearrange("p (x h d) -> p x h d", x=2, h=8)[:, :, :, 0:ROPE],
                   spread(gpre[:, :, :].rearrange("p x (o d) -> p x o d", o=1), [P, 2, 8, ROPE]), ALU.mult).then_inc(s["rope_in"], 1)
                e.wait_ge(s["rope_in"], t + 1)
                cos, sin = (spread(sincos[:, j, t, :].rearrange("p (o f) -> p o f", o=1), [P, 16, HALF]) for j in range(2))
                for o, a, b in zip(prod, (x1, x2, x2, x1), (cos, sin, cos, sin)):
                    last = tt(o, a, b, ALU.mult)
                last.then_inc(s["rope_prod"], 1)
                e.wait_ge(s["rope_prod"], t + 1)
                tt(qk[:, :, 0:HALF], prod[0], prod[1], ALU.subtract)
                tt(qk[:, :, HALF:ROPE], prod[2], prod[3], ALU.add).then_inc(s["rope_done"], 1)

            e.wait_ge(s["mods_ps"], 1)
            v.tensor_copy(S2[:, :], bank(0)[:, 0:KT])
            stt(A2[:, :], bank(0)[:, KT:2 * KT], 1.0, gcols[:, KT:2 * KT], ALU.add, ALU.mult).then_inc(s["mods_col"], 1)
            e.wait_ge(s["pad_st"], 64)
            for t in range(NT):
                e.wait_ge(s["qk_tr"], t + 1)
                tsc(kT[:, :, t * P:(t + 1) * P], bank(5 + 2 * (t % 2)).rearrange("p (h t) -> p h t", h=NH),
                    gcols[:, 17:18], ALU.mult).then_inc(s["kT_done"], 1)

            e.wait_ge(s["kT_done"], NT)
            v.tensor_copy(ks, kT[:, 0, :]).then_inc(s["head_staged"], 1)

            e.wait_ge(s["lam_done"], 2)
            score_v = PS[:, 0:4, :].rearrange("p (c b) n -> p c (b n)", c=2)
            with e.Fori(0, NH) as h:
                def row_max(i):
                    e.wait_ge(s["scores_ready"], h * NT + i + 2)
                    v.tensor_reduce(att_mx[:, i % 2, :], score_v[:, :, 0:(i + 1) * P], AX.X, ALU.max).then_inc(s["max_ready"], 1)
                    e.wait_ge(s["max_ready"], h * NT + i + 1)
                    tsc(att_nm[:, i % 2, :], att_mx[:, i % 2, :], -DK ** -0.5, ALU.mult).then_inc(s["nmax_ready"], 1)

                def combine(i):
                    n = (i + 1) * P
                    e.wait_ge(s["exp_done"], h * NT + i + 2)
                    e.wait_ge(s["att_o_done"], h * NT + i + 1)
                    v.reciprocal(att_rc[:, i % 2, 0:2], att_sum[:, i % 2, :]).then_inc(s["att_r"], 1)
                    e.wait_ge(s["att_r"], h * NT + i + 1)
                    stt(att_rc[:, i % 2, 2:3], att_rc[:, i % 2, 1:2], att_sum[:, i % 2, 0:1], lam[:, 4:5],
                        ALU.mult, ALU.mult).then_inc(s["att_nr"], 1)
                    e.wait_ge(s["att_nr"], h * NT + i + 1)
                    e.wait_ge(s["att_tr"], h * NT + i + 1)
                    stt(attn[i % 2][:, 0:n], E[:, i % 2, 1, 0:n], att_rc[:, i % 2, 2:3], E[:, i % 2, 0, 0:n],
                        ALU.mult, ALU.add).then_inc(s["att_a"], 1)

                def finish(i):
                    e.wait_ge(s["att_o"], h * NT + i + 3)
                    tsc(qT[:, ds(h, 1), i * P:(i + 1) * P].rearrange("p o d -> p (o d)"), bank(6)[:, 0:DV], att_rc[:, i % 2, 0:1], ALU.mult).then_inc(s["att_o_done"], 1)

                row_max(0)
                for i in range(NT):
                    if i + 1 < NT:
                        row_max(i + 1)
                    combine(i)
                    if i >= 1:
                        finish(i - 1)
                finish(NT - 1)

            e.wait_ge(s["proj_free"], 4 + 6 * NT)
            v.tensor_copy(U[:, :, 1024:1536], gv_tmp).then_inc(s["gv_moved"], 1)
            e.wait_ge(s["out_sd"], 1)
            v.reciprocal(sso[:, 0, :], sso[:, 0, :]).then_inc(s["out_rs"], 1)
            e.wait_ge(s["out_rs"], 1)
            rs = sso[:, 0, :].rearrange("p (h t o) -> p h t o", h=NH, o=1)
            for t in range(NT):
                tt(o_att[:, :, t, :], o_att[:, :, t, :], spread(rs[:, :, t, :], [P, NH, DV]), ALU.mult).then_inc(s["ob_norm"], 1)

            e.wait_ge(s["z_step"], 3)
            stt(sp, bank(0, 4), 0.0, sp, ALU.min, ALU.subtract).then_inc(s["g_done"], 1)
            e.wait_ge(s["dec_done"], 1)
            e.wait_ge(s["gla_zero"], 1)

            def gla_scale(t, u):
                e.wait_ge(s["gla_sc"], t + 1)
                stt(qin[u], U[:, t, 512:768], DK ** -0.5, EB[:, t, :], ALU.mult, ALU.mult)
                tt(kin[u], U[:, t, 768:1024], ENB[:, t, :], ALU.mult)
                tt(kdc[u], U[:, t, 768:1024], EKD[:, t, :], ALU.mult).then_inc(s["gla_in"], 1)

            def gla_state(t, u):
                v.tensor_copy(dcur[:, u, :], dec[:, ds(t * 4, 4)]).then_inc(s["gla_dec"], 1)
                e.wait_ge(s["gla_dec"], t + 1)
                e.wait_ge(s["gla_sc"], t + 3)
                e.wait_ge(s["gla_out_state"], t + 1)
                for pr in range(2):
                    last = stt(S_mid[u][:, pr, :], S_in[u][:, pr, :], dcur[:, u, 2 * pr:2 * pr + 1],
                               bank(3)[:, pr * DV:(pr + 1) * DV], ALU.mult, ALU.add)
                last.then_inc(s["gla_mid"], 1)
                e.wait_ge(s["gla_mid"], t + 1)
                e.wait_ge(s["gla_o"], t + 2)
                for pr in range(2):
                    last = stt(S_in[1 - u][:, pr, :], S_mid[u][:, pr, :], dcur[:, u, 2 * pr + 1:2 * pr + 2],
                               bank(4)[:, pr * DV:(pr + 1) * DV], ALU.mult, ALU.add)
                last.then_inc(s["gla_out_state"], 1)

            def gla_mask(t, u):
                wait_apart(e, (s["gla_att"], t + 1))
                for hd in range(NH):
                    last = v.copy_predicated(attS[u][:, hd, :], tri[:, :].bitcast(U32),
                                             bank(1 + hd % 2)[:, (hd // 2) * P:(hd // 2 + 1) * P])
                last.then_inc(s["gla_attS"], 1)

            gla_scale(0, 0)
            with e.Fori(0, NT // 2 - 1) as i:
                for u in range(2):
                    t = 2 * i + u
                    gla_scale(t + 1, 1 - u)
                    gla_state(t, u)
                    gla_mask(t, u)
            gla_scale(NT - 1, 1)
            for t in (NT - 2, NT - 1):
                gla_state(t, t % 2)
                gla_mask(t, t % 2)

            with e.Fori(0, NT // 2) as i:
                for u in range(2):
                    e.wait_ge(s["oa_sq"], 2 * i + u + 1)
                    v.tensor_reduce(sso[:, 1, ds((2 * i + u) * NH, NH)], R4[:, HW * u:HW * (u + 1)].rearrange("p (c d) -> p c d", d=DV),
                                    AX.X, ALU.add).then_inc(s["oa_sum"], 1)
            e.wait_ge(s["out_sd"], 2)
            v.reciprocal(sso[:, 1, :], sso[:, 1, :]).then_inc(s["out_rs"], 1)
            e.wait_ge(s["out_rs"], 2)
            e.wait_ge(s["oa_silu"], 1)
            with e.Fori(0, NT) as t:
                o = U[:, t, 1024:1536].rearrange("p (c d) -> p c d", d=DV)
                tt(o, o, spread(sso[:, 1, ds(t * NH, NH)].rearrange("p (c o) -> p c o", o=1), [P, NH, DV]), ALU.mult).then_inc(s["oa_n1"], 1)
                e.wait_ge(s["oa_n1"], t + 1)
                tt(U[:, t, 1024:1536], U[:, t, 1024:1536], U[:, t, 0:HW], ALU.mult).then_inc(s["oa_norm"], 1)

            e.wait_ge(s["oaT_done"], NT)
            e.wait_ge(s["early_sig"], 8)
            for n, (f, half) in enumerate(((1, 0), (1, 1), (0, 0), (0, 1))):
                e.wait_ge(s["g_mm"], n + 1)
                ga, gb = early[f][0][half], early[f][1][half]
                tt(ga, ga, bank(4 * half + 2 - 2 * f), ALU.mult)
                tt(gb, gb, bank(4 * half + 3 - 2 * f), ALU.mult).then_inc(s["g_prod"], 1)
                e.wait_ge(s["g_prod"], n + 1)
                tt(mT[:, f, half * 512:(half + 1) * 512], ga, gb, ALU.add).then_inc(s["g_free"], 1)
            with e.Fori(2, KT) as f:
                for half in range(2):
                    n = 2 * f + half
                    e.wait_ge(s["g_sig"], n - 3)
                    for x in range(2):
                        last = tt(sig[:, 2 * half + x, :], sig[:, 2 * half + x, :], bank(4 * half + 2 + x), ALU.mult)
                    last.then_inc(s["g_prod"], 1)
                    e.wait_ge(s["g_prod"], n + 1)
                    tt(mT[:, f, half * 512:(half + 1) * 512], sig[:, 2 * half, :], sig[:, 2 * half + 1, :], ALU.add).then_inc(s["g_free"], 1)

            with e.Fori(0, NT // 2) as i:
                for u in range(2):
                    t = 2 * i + u
                    e.wait_ge(s["mo_mm"], t + 3)
                    e.wait_ge(xn_st[u], 16 * (i + 1))
                    e.wait_ge(s["h2_tr"], t + 1)
                    tt(xn[u], bank(2 * u, 2), gate[:, 0, :], ALU.mult).then_inc(s["mo_gated"], 1)
                    e.wait_ge(s["mo_gated"], t + 3)
                    e.wait_ge(xh_ld[u], 16 * (i + 1))
                    tt(xh[u], xh[u], xn[u], ALU.add).then_inc(s["x1_ready"], 1)
                    e.wait_ge(s["x1_sd"], t + 1)
                    v.reciprocal(stat[:, 2, u:u + 1], stat[:, 3, u:u + 1]).then_inc(s["x1_rs"], 1)
                    e.wait_ge(s["h2_tr"], t + 3)
                    for k in range(4):
                        last = tsc(h2T[u][:, k, :], bank(4)[:, k * P:(k + 1) * P],
                                   A2[:, k:k + 1], ALU.mult, S2[:, k:k + 1], ALU.add)
                    last.then_inc(s["h2_evd"], 1)
                    e.wait_ge(s["rt_mm"], t + 3)
                    tt(logits[:, t, :], bank(6)[:, 0:NR], rbias[:, :], ALU.add).then_inc(s["rt_done"], 1)

            n_rt = [0]

            def rt(ins):
                n_rt[0] += 1
                ins.then_inc(s["rt_step"], 1)
                e.wait_ge(s["rt_step"], n_rt[0])

            def over(a, n):
                return spread(a.rearrange("p (t o) -> p t o", o=1), [P, NT, n])

            def first_max(x, n, m, eq, ids, oh):
                rt(v.tensor_reduce(m, x, AX.X, ALU.max))
                rt(tt(eq, x, over(m, n), ALU.is_equal))
                ids_b = spread(iota_e[:, 0:n].rearrange("p (o e) -> p o e", o=1), [P, NT, n])
                rt(stt(eq, eq, -float(NE), ids_b, ALU.mult, ALU.add))
                rt(v.tensor_reduce(ids, eq, AX.X, ALU.min))
                rt(tt(oh, eq, over(ids, n), ALU.is_equal))

            e.wait_ge(s["rt_done"], 1 + NT)
            lg = logits[:, :, 0:NG]
            le = logits[:, :, NG:NR]
            first_max(lg, NG, gm, eq_g, ids, oh_g)
            tt(rt_gd, lg, over(gm, NG), ALU.subtract).then_inc(s["rt_diff"], 1)
            rt(tsc(oh_g, oh_g, -1.0, ALU.add, -NEG, ALU.mult))
            rt(tt(le.rearrange("p t (g x) -> p t g x", g=NG), le.rearrange("p t (g x) -> p t g x", g=NG),
                  spread(oh_g.rearrange("p t (g o) -> p t g o", o=1), [P, NT, NG, EPG]), ALU.add))
            first_max(le, NE, m1, eq_e, ids, oh1)
            rt(stt(le, oh1, 2 * NEG, le, ALU.mult, ALU.add))
            first_max(le, NE, m2, eq_e, ids, oh2)
            tt(rt_d[:, 0, :], m2, m1, ALU.subtract).then_inc(s["rt_diff"], 1)
            rt(tt(choice_b[:, 0:NT, :], oh1, oh2, ALU.add))
            rt(v.memset(choice_b[:, NT, :], 0.0))
            for t in range(NT):
                rt(tt(choice_b[:, NT + 1 + t, :], choice_b[:, NT + t, :], choice_b[:, t, :], ALU.add))
            e.sem_inc(s["rt_m"], 1)
            e.wait_ge(s["rt_exp"], 1)
            rt(v.tensor_reduce(gsum, rt_gd, AX.X, ALU.add))
            rt(v.reciprocal(p_top, gsum))
            e.wait_ge(s["rt_exp"], 2)
            rt(tsc(gsum, rt_d[:, 1, :], 1.0, ALU.add))
            rt(v.reciprocal(gsum, gsum))
            rt(tt(gsum, gsum, p_top, ALU.mult))
            rt(v.tensor_copy(wts[:, 0:NT], gsum))
            rt(tt(wts[:, NT:2 * NT], gsum, rt_d[:, 1, :], ALU.mult))
            e.wait_ge(s["rt_sums_mm"], 1)
            rt(v.tensor_copy(cnt, bank(1)[:, 0:NE]))
            big = R2[:, 4096:4096 + NE * NE]
            cmp = big[:, 0:NE * (NT - 1)].rearrange("p (x n) -> p x n", n=NT - 1)
            rt(tt(cmp, spread(cnt.rearrange("p (x o) -> p x o", o=1), [P, NE, NT - 1]),
                  spread(thr128[:, :].rearrange("p (o n) -> p o n", o=1), [P, NE, NT - 1]), ALU.is_gt))
            rt(v.tensor_reduce(extra, cmp, AX.X, ALU.add))
            sq = big.rearrange("p (x y) -> p x y", y=NE)
            e.wait_ge(s["mask0"], 6)
            rt(tt(sq, spread(extra.rearrange("p (o y) -> p o y", o=1), [P, NE, NE]), earlier, ALU.mult))
            rt(v.tensor_reduce(ovb, sq, AX.X, ALU.add))
            rt(stt(delta, ovb, float(NE - 1), pos_e[:, :], ALU.add, ALU.subtract))
            rt(tsc(delta, delta, float(P), ALU.mult))
            rank = bank(0)[:, 0:NT * NE].rearrange("p (t x) -> p t x", x=NE)
            rt(tsc(eq_e, rank, float(P), ALU.is_ge))
            rt(tt(eq_e, eq_e, spread(delta.rearrange("p (o x) -> p o x", o=1), [P, NT, NE]), ALU.mult))
            rt(tt(eq_e, eq_e, rank, ALU.add))
            rt(tsc(delta, pos_e[:, :], float(P), ALU.mult))
            rt(tt(eq_e, eq_e, spread(delta.rearrange("p (o x) -> p o x", o=1), [P, NT, NE]), ALU.add))
            for k, oh in enumerate((oh1, oh2)):
                rt(tt(oh, oh, eq_e, ALU.mult))
                rt(v.tensor_reduce(dest[:, k * NT:(k + 1) * NT], oh, AX.X, ALU.add))
            e.wait_ge(s["mask0"], 8)
            for k in range(2):
                c = slice(k * NT, (k + 1) * NT)
                rt(tt(past[:, c], spread(dest[:, c].rearrange("p (c o) -> p c o", o=1), [P, NT, NB1]),
                      spread(starts.rearrange("p (o b) -> p o b", o=1), [P, NT, NB1]), ALU.is_ge))
                rt(v.tensor_reduce(past_n[:, c], past[:, c], AX.X, ALU.add))
                rt(stt(past_n[:, c], past_n[:, c], -float(P), dest[:, c], ALU.mult, ALU.add))
                tt(d1[:, c], spread(past_n[:, c].rearrange("p (c o) -> p c o", o=1), [P, NT, P]),
                   spread(slot_row.rearrange("p (o n) -> p o n", o=1), [P, NT, P]), ALU.is_equal)
                rt(tt(d2[:, c, 2, :], past[:, c, 0:NBLK], past[:, c, 1:NB1], ALU.subtract))
                for x, col in ((0, tok_col), (1, wts)):
                    last = tt(d2[:, c, x, :], d2[:, c, 2, :],
                              spread(col[:, c].rearrange("p (c o) -> p c o", o=1), [P, NT, NBLK]), ALU.mult)
                last.then_inc(s["slots_in"], 1)
            e.wait_ge(s["rt_sums_mm"], 2)
            rt(v.tensor_copy(tab_w, bank(2)[:, NBLK:2 * NBLK]))
            rt(tsc(tab_gap, bank(2)[:, 2 * NBLK:3 * NBLK], -1.0, ALU.mult, 1.0, ALU.add))
            rt(tt(tab_gap, tab_gap, pad_tok, ALU.mult))
            rt(tt(tab_tok, tab_gap, bank(2)[:, 0:NBLK], ALU.add))
            e.sem_inc(s["tab_done"], 1)
            rt(tt(ovb, ovb, extra, ALU.add))
            ends = big[:, 0:MAXOV * NE].rearrange("p (j x) -> p j x", x=NE)
            rt(tt(ends, spread(ovb.rearrange("p (o x) -> p o x", o=1), [P, MAXOV, NE]),
                  spread(thr[:, :].rearrange("p (j o) -> p j o", o=1), [P, MAXOV, NE]), ALU.is_le))
            rt(v.tensor_reduce(ovf_f[:, 0:MAXOV], ends, AX.X, ALU.add))
            rt(tsc(ovf_f[:, 0:MAXOV], ovf_f[:, 0:MAXOV], float(NE - 1), ALU.min))
            rt(v.tensor_copy(ovf_f[:, MAXOV:MAXOV + 1], ovb[:, NE - 1:NE]))
            v.tensor_copy(ovf[:, :], ovf_f).then_inc(s["ovf_ready"], 1)

            def rows_read(n, u):
                e.wait_ge(s["m_tr"], n + 3)
                for k in range(4):
                    last = tsc(xT[u][:, k, :], bank(0)[:, k * P:(k + 1) * P],
                               A2[:, k:k + 1], ALU.mult, S2[:, k:k + 1], ALU.add)
                last.then_inc(s["m_evd"], 1)

            def hidden(n):
                e.wait_ge(s["m_silu"], n + 1)
                e.wait_ge(s["m2_tr"], n + 1)
                tt(hh, sg, bank(3), ALU.mult).then_inc(s["m_hh"], 1)

            def weighted(n, u):
                v.tensor_copy(wt[:, u:u + 1], tab_w[:, ds(n, 1)]).then_inc(s["m_wt"], 1)
                e.wait_ge(s["m_wt"], n + 1)
                e.wait_ge(s["m2_mm"], n + 2)
                e.wait_ge(s["tis_ready"], n + 1)
                stt(yb[u], bank(6, 2), wt[:, u:u + 1], gate[:, 1, :], ALU.mult, ALU.mult).then_inc(s["m_y"], 1)

            rows_read(0, 0)
            hidden(0)
            rows_read(1, 1)
            with e.Fori(0, NE // 2 - 1) as i:
                for u in (1, 0):
                    n = 2 * i + 2 - u
                    hidden(n)
                    rows_read(n + 1, 1 - u)
                    weighted(n - 1, 1 - u)
            hidden(NE - 1)
            weighted(NE - 2, 0)
            weighted(NE - 1, 1)
            e.wait_ge(s["ovf_ready"], 1)
            n_ov = e.value_load(ovf[0:1, MAXOV:MAXOV + 1], min_val=0, max_val=MAXOV)
            with e.If(n_ov > 0):
                with e.Fori(0, n_ov) as j:
                    rows_read(NE + j, 0)
                    hidden(NE + j)
                    weighted(NE + j, 0)


_INS = ["x", "c", "positions", "ada_w", "ada_b", "norm1_g", "norm2_g", "w_in", "gla_alpha_up", "gla_alpha_b",
        "gla_out_g", "diff_q_g", "diff_k_g", "diff_lq1", "diff_lk1", "diff_lq2", "diff_lk2", "diff_out_g",
        "w_branch_a", "w_branch_b", "w_out", "router_group_w", "router_group_b", "router_expert_w",
        "router_expert_b", "expert_w1", "expert_w3", "expert_w2"]


def kernel(**inputs):
    import concourse.bacc as bacc
    from concourse.bass_utils import run_bass_kernel_spmd

    nc = bacc.Bacc("TRN2", target_bir_lowering=False, num_devices=1)
    arrays, io = {}, {}
    for name in _INS:
        a = np.ascontiguousarray(inputs[name])[0]
        arrays[f"in_{name}"] = a
        io[name] = nc.dram_tensor(f"in_{name}", a.shape, mybir.dt.from_np(a.dtype), kind="ExternalInput").ap()
    out = nc.dram_tensor("out_rows", (T + PAD, D), F32, kind="ExternalOutput").ap()
    build(nc, io, out)
    r = run_bass_kernel_spmd(nc, [arrays], core_ids=[0])
    return r.results[0]["out_rows"][:T].reshape(1, T, D)
```
